# Optimizing a Trainium2 kernel written in Bass

```python
import math
import jax, jax.numpy as jnp
from jax import lax
import numpy as np

D_MODEL = 1024
BATCH = 1
SEQ = 512
DEPTH = 1

CHUNK = 64
N_META = 16
Q_BLOCK = 128
SB_HEADS = 8
SB_HEAD_DIM = 64
SB_WIDTH = SB_HEADS * SB_HEAD_DIM
MLA_HEADS = 8
MLA_Q_LORA = 384
MLA_KV_LORA = 256
MLA_NOPE = 64
MLA_ROPE = 32
MLA_V = 64
MLA_WIDTH = MLA_HEADS * MLA_V
ROPE_THETA = 10000.0
N_BRANCH = 2
IN_COLS = 3 * SB_WIDTH + MLA_Q_LORA + MLA_KV_LORA + MLA_ROPE + N_BRANCH * D_MODEL
D_FF = 2816
EPS = 1e-6
NEG_INF = -1e30
PAD_CHUNK_ID = 2 ** 30


def rmsnorm(x, g):
    xf = x.astype(jnp.float32)
    y = xf * lax.rsqrt(jnp.mean(xf * xf, axis=-1, keepdims=True) + EPS)
    return (y * g.astype(jnp.float32)).astype(x.dtype)

def swiglu(h, w_gate, w_up, w_down):
    return (jax.nn.silu(h @ w_gate) * (h @ w_up)) @ w_down

def rope(x, pos):
    half = x.shape[-1] // 2
    inv = ROPE_THETA ** (-jnp.arange(half, dtype=jnp.float32) / half)
    ang = pos[:, None] * inv[None, :]
    cos = jnp.cos(ang).astype(x.dtype)
    sin = jnp.sin(ang).astype(x.dtype)
    x1, x2 = x[..., :half], x[..., half:]
    return jnp.concatenate([x1 * cos - x2 * sin, x1 * sin + x2 * cos], axis=-1)

def to_heads(t, n_heads):
    b, l, _ = t.shape
    return t.reshape(b, l, n_heads, -1).transpose(0, 2, 1, 3)

def from_heads(t):
    b, h, l, d = t.shape
    return t.transpose(0, 2, 1, 3).reshape(b, l, h * d)

def chunk_end(pos):
    if pos < N_META:
        return N_META
    return N_META + ((pos - N_META) // CHUNK + 1) * CHUNK

def stick_breaking_attention(q, k, v):
    lp, d = q.shape[2], q.shape[3]
    scale = d ** -0.5
    outs = []
    for blk in range(lp // Q_BLOCK):
        q0, q1 = blk * Q_BLOCK, (blk + 1) * Q_BLOCK
        z = jnp.einsum('bhtd,bhsd->bhts', q[:, :, q0:q1], k[:, :, :q1]).astype(jnp.float32) * scale
        strict = jnp.arange(q1)[None, :] < jnp.arange(q0, q1)[:, None]
        log_1m = jnp.where(strict, jax.nn.log_sigmoid(-z), 0.0)
        csum = jnp.cumsum(log_1m, axis=-1)
        log_a = jax.nn.log_sigmoid(z) + csum[..., -1:] - csum
        a = jnp.where(strict, jnp.exp(log_a), 0.0)
        outs.append(jnp.einsum('bhts,bhsd->bhtd', a.astype(v.dtype), v[:, :, :q1]))
    return jnp.concatenate(outs, axis=2)

def latent_attention(q_nope, q_rope, k_nope, k_rope, v, cid):
    lp = q_nope.shape[2]
    scale = (MLA_NOPE + MLA_ROPE) ** -0.5
    outs = []
    for blk in range(lp // Q_BLOCK):
        q0, q1 = blk * Q_BLOCK, (blk + 1) * Q_BLOCK
        kend = min(lp, chunk_end(q1 - 1))
        s = (jnp.einsum('bhtd,bhsd->bhts', q_nope[:, :, q0:q1], k_nope[:, :, :kend])
             + jnp.einsum('bhtd,bsd->bhts', q_rope[:, :, q0:q1], k_rope[:, :kend]))
        s = s.astype(jnp.float32) * scale
        mask = cid[None, :kend] <= cid[q0:q1, None]
        p = jax.nn.softmax(jnp.where(mask, s, NEG_INF), axis=-1)
        outs.append(jnp.einsum('bhts,bhsd->bhtd', p.astype(v.dtype), v[:, :, :kend]))
    return jnp.concatenate(outs, axis=2)

def hybrid_mixer(u, w_in, b_gate, q_norm_g, w_uq, kv_norm_g, w_ukv, w_sb_o, w_mla_o, w_out):
    bsz, l, _ = u.shape
    lp = -(-l // Q_BLOCK) * Q_BLOCK
    up = jnp.pad(u, ((0, 0), (0, lp - l), (0, 0)))
    proj = up @ w_in
    sizes = [SB_WIDTH, SB_WIDTH, SB_WIDTH, MLA_Q_LORA, MLA_KV_LORA, MLA_ROPE, N_BRANCH * D_MODEL]
    idx = np.cumsum(sizes)[:-1].tolist()
    sb_q, sb_k, sb_v, c_q, c_kv, k_r, gate_pre = jnp.split(proj, idx, axis=-1)

    pos = jnp.arange(lp)
    cid = jnp.where(pos < N_META, 0, 1 + (pos - N_META) // CHUNK)
    cid = jnp.where(pos < l, cid, PAD_CHUNK_ID)
    posf = pos.astype(jnp.float32)

    y_sb = stick_breaking_attention(to_heads(sb_q, SB_HEADS), to_heads(sb_k, SB_HEADS),
                                    to_heads(sb_v, SB_HEADS))
    y_sb = from_heads(y_sb) @ w_sb_o

    q = jnp.einsum('bld,dhe->bhle', rmsnorm(c_q, q_norm_g), w_uq)
    q_nope, q_rope = q[..., :MLA_NOPE], rope(q[..., MLA_NOPE:], posf)
    kv = jnp.einsum('bld,dhe->bhle', rmsnorm(c_kv, kv_norm_g), w_ukv)
    k_nope, v = kv[..., :MLA_NOPE], kv[..., MLA_NOPE:]
    k_rope = rope(k_r, posf)
    y_mla = latent_attention(q_nope, q_rope, k_nope, k_rope, v, cid)
    y_mla = from_heads(y_mla) @ w_mla_o

    g = jax.nn.sigmoid(gate_pre + b_gate)
    g_sb, g_mla = g[..., :D_MODEL], g[..., D_MODEL:]
    out = (g_sb * y_sb + g_mla * y_mla) @ w_out
    return out[:, :l]

def first_inputs(seed: int = 0) -> dict:
    key = jax.random.key(seed)
    ks = jax.random.split(key, 24)

    def w(k, shape, fan_in):
        return jax.random.normal(k, shape, jnp.float32) * fan_in ** -0.5

    def gain(k, n):
        return 1.0 + 0.02 * jax.random.normal(k, (DEPTH, n), jnp.float32)

    return {
        "x": jax.random.normal(ks[0], (BATCH, SEQ, D_MODEL), jnp.float32),
        "meta_tokens": jax.random.normal(ks[1], (N_META, D_MODEL), jnp.float32),
        "ffn1_pre_g": gain(ks[2], D_MODEL),
        "ffn1_w_gate": w(ks[3], (DEPTH, D_MODEL, D_FF), D_MODEL),
        "ffn1_w_up": w(ks[4], (DEPTH, D_MODEL, D_FF), D_MODEL),
        "ffn1_w_down": w(ks[5], (DEPTH, D_FF, D_MODEL), D_FF),
        "ffn1_post_g": gain(ks[6], D_MODEL),
        "mix_pre_g": gain(ks[7], D_MODEL),
        "w_in": w(ks[8], (DEPTH, D_MODEL, IN_COLS), D_MODEL),
        "b_gate": 0.02 * jax.random.normal(ks[9], (DEPTH, N_BRANCH * D_MODEL), jnp.float32),
        "q_norm_g": gain(ks[10], MLA_Q_LORA),
        "w_uq": w(ks[11], (DEPTH, MLA_Q_LORA, MLA_HEADS, MLA_NOPE + MLA_ROPE), MLA_Q_LORA),
        "kv_norm_g": gain(ks[12], MLA_KV_LORA),
        "w_ukv": w(ks[13], (DEPTH, MLA_KV_LORA, MLA_HEADS, MLA_NOPE + MLA_V), MLA_KV_LORA),
        "w_sb_o": w(ks[14], (DEPTH, SB_WIDTH, D_MODEL), SB_WIDTH),
        "w_mla_o": w(ks[15], (DEPTH, MLA_WIDTH, D_MODEL), MLA_WIDTH),
        "w_out": w(ks[16], (DEPTH, D_MODEL, D_MODEL), D_MODEL),
        "mix_post_g": gain(ks[17], D_MODEL),
        "ffn2_pre_g": gain(ks[18], D_MODEL),
        "ffn2_w_gate": w(ks[19], (DEPTH, D_MODEL, D_FF), D_MODEL),
        "ffn2_w_up": w(ks[20], (DEPTH, D_MODEL, D_FF), D_MODEL),
        "ffn2_w_down": w(ks[21], (DEPTH, D_FF, D_MODEL), D_FF),
        "ffn2_post_g": gain(ks[22], D_MODEL),
    }

def first_block(x, meta_tokens, ffn1_pre_g, ffn1_w_gate, ffn1_w_up, ffn1_w_down, ffn1_post_g,
              mix_pre_g, w_in, b_gate, q_norm_g, w_uq, kv_norm_g, w_ukv, w_sb_o, w_mla_o,
              w_out, mix_post_g, ffn2_pre_g, ffn2_w_gate, ffn2_w_up, ffn2_w_down, ffn2_post_g):
    bsz = x.shape[0]
    meta = jnp.broadcast_to(meta_tokens[None].astype(x.dtype), (bsz, N_META, x.shape[-1]))
    h = jnp.concatenate([meta, x], axis=1)
    for l in range(DEPTH):
        f = swiglu(rmsnorm(h, ffn1_pre_g[l]), ffn1_w_gate[l], ffn1_w_up[l], ffn1_w_down[l])
        h = h + 0.5 * rmsnorm(f, ffn1_post_g[l])
        m = hybrid_mixer(rmsnorm(h, mix_pre_g[l]), w_in[l], b_gate[l], q_norm_g[l], w_uq[l],
                         kv_norm_g[l], w_ukv[l], w_sb_o[l], w_mla_o[l], w_out[l])
        h = h + rmsnorm(m, mix_post_g[l])
        f = swiglu(rmsnorm(h, ffn2_pre_g[l]), ffn2_w_gate[l], ffn2_w_up[l], ffn2_w_down[l])
        h = h + 0.5 * rmsnorm(f, ffn2_post_g[l])
    return h[:, N_META:]


DEPTH_2 = 2

PLE_DIM = 256
N_EVEN = (DEPTH_2 + 1) // 2
N_ODD = DEPTH_2 // 2
RG_WIDTH = 512
RG_BLOCKS = 8
RG_BLOCK = RG_WIDTH // RG_BLOCKS
RG_CONV = 4
RG_C = 8.0
ML_HEADS = 4
ML_HEAD_DIM = 128
ML_WIDTH = ML_HEADS * ML_HEAD_DIM
ML_CONV = 4
ML_CHUNK = 64
HY_IN = 2 * RG_WIDTH + 4 * ML_WIDTH + 2 * ML_HEADS
HY_MIX = RG_WIDTH + ML_WIDTH
AT_HEADS = 16
AT_KV_HEADS = 4
AT_HEAD_DIM = 64
WINDOW = 128
AT_QKV = (AT_HEADS + 2 * AT_KV_HEADS) * AT_HEAD_DIM
FF_DIM = 3 * D_MODEL
FF_CONV = 3


def rms_norm(x, g):
    xf = x.astype(jnp.float32)
    y = xf * lax.rsqrt(jnp.mean(xf * xf, axis=-1, keepdims=True) + EPS)
    return (y * g.astype(jnp.float32)).astype(x.dtype)

def causal_dwconv(x, w, b):
    k_w = w.shape[0]
    s = x.shape[1]
    xp = jnp.pad(x, ((0, 0), (k_w - 1, 0), (0, 0)))
    y = xp[:, 0:s] * w[0]
    for j in range(1, k_w):
        y = y + xp[:, j:j + s] * w[j]
    return y + b

def _linear_recurrence_combine(left, right):
    a_l, b_l = left
    a_r, b_r = right
    return a_l * a_r, a_r * b_l + b_r

def rg_lru(x, w_a, b_a, w_x, b_x, lam):
    f32 = jnp.float32
    bsz, s, _ = x.shape
    xf = x.astype(f32)
    xb = xf.reshape(bsz, s, RG_BLOCKS, RG_BLOCK)
    r = jax.nn.sigmoid(jnp.einsum('bsni,nij->bsnj', xb, w_a.astype(f32)).reshape(bsz, s, RG_WIDTH) + b_a.astype(f32))
    i = jax.nn.sigmoid(jnp.einsum('bsni,nij->bsnj', xb, w_x.astype(f32)).reshape(bsz, s, RG_WIDTH) + b_x.astype(f32))
    log_a = -RG_C * r * jax.nn.softplus(-lam.astype(f32))
    a = jnp.exp(log_a)
    u = jnp.sqrt(-jnp.expm1(2.0 * log_a)) * (i * xf)
    _, h = lax.associative_scan(_linear_recurrence_combine, (a, u), axis=1)
    return h

def mlstm_chunkwise(q, k, v, i_pre, f_pre):
    f32 = jnp.float32
    bsz, s, nh, dh = q.shape
    nc = s // ML_CHUNK

    def to_chunks(t):
        return t.astype(f32).reshape(bsz, nc, ML_CHUNK, nh, dh).transpose(0, 3, 1, 2, 4)

    def gate_chunks(t):
        return t.astype(f32).reshape(bsz, nc, ML_CHUNK, nh).transpose(0, 3, 1, 2)

    qc = to_chunks(q)
    kc = to_chunks(k) * (dh ** -0.5)
    vc = to_chunks(v)
    log_i = gate_chunks(i_pre)
    log_f = jax.nn.log_sigmoid(gate_chunks(f_pre))
    b = jnp.cumsum(log_f, axis=-1)
    b_last = b[..., -1]

    g = b_last[..., None] - b + log_i
    m_loc = jnp.max(g, axis=-1)
    w_loc = jnp.exp(g - m_loc[..., None])
    c_loc = jnp.einsum('bhcl,bhcld,bhcle->bhcde', w_loc, kc, vc)
    n_loc = jnp.einsum('bhcl,bhcld->bhcd', w_loc, kc)

    def step(carry, inp):
        c_st, n_st, m_st = carry
        c_l, n_l, m_l, b_l = inp
        m_new = jnp.maximum(b_l + m_st, m_l)
        a_prev = jnp.exp(b_l + m_st - m_new)
        a_loc = jnp.exp(m_l - m_new)
        c_new = a_prev[..., None, None] * c_st + a_loc[..., None, None] * c_l
        n_new = a_prev[..., None] * n_st + a_loc[..., None] * n_l
        return (c_new, n_new, m_new), (c_st, n_st, m_st)

    init = (jnp.zeros((bsz, nh, dh, dh), f32), jnp.zeros((bsz, nh, dh), f32), jnp.full((bsz, nh), -jnp.inf, f32))
    xs = (jnp.moveaxis(c_loc, 2, 0), jnp.moveaxis(n_loc, 2, 0), jnp.moveaxis(m_loc, 2, 0), jnp.moveaxis(b_last, 2, 0))
    _, (c_prev, n_prev, m_prev) = lax.scan(step, init, xs)
    c_prev = jnp.moveaxis(c_prev, 0, 2)
    n_prev = jnp.moveaxis(n_prev, 0, 2)
    m_prev = jnp.moveaxis(m_prev, 0, 2)

    idx = jnp.arange(ML_CHUNK)
    causal = idx[:, None] >= idx[None, :]
    d_log = b[..., :, None] - b[..., None, :] + log_i[..., None, :]
    d_log = jnp.where(causal, d_log, -jnp.inf)
    inter_log = b + m_prev[..., None]
    m_t = jnp.maximum(inter_log, jnp.max(d_log, axis=-1))
    w_intra = jnp.exp(d_log - m_t[..., None])
    a_inter = jnp.exp(inter_log - m_t)
    s_qk = jnp.einsum('bhctd,bhcsd->bhcts', qc, kc) * w_intra
    num = jnp.einsum('bhcts,bhcse->bhcte', s_qk, vc) + a_inter[..., None] * jnp.einsum('bhctd,bhcde->bhcte', qc, c_prev)
    den = jnp.sum(s_qk, axis=-1) + a_inter * jnp.einsum('bhctd,bhcd->bhct', qc, n_prev)
    h = num / jnp.maximum(jnp.abs(den), jnp.exp(-m_t))[..., None]
    return h.transpose(0, 2, 3, 1, 4).reshape(bsz, s, nh, dh)

def rglru_mlstm_mixer(h, w_in, b_in, rg_conv_w, rg_conv_b, rg_w_a, rg_b_a, rg_w_x, rg_b_x, rg_lambda,
                      ml_conv_w, ml_conv_b, ml_norm, w_out):
    f32 = jnp.float32
    bsz, s, _ = h.shape
    z = h @ w_in + b_in
    cuts = [RG_WIDTH, 2 * RG_WIDTH, 2 * RG_WIDTH + ML_WIDTH, 2 * RG_WIDTH + 2 * ML_WIDTH,
            2 * RG_WIDTH + 3 * ML_WIDTH, 2 * RG_WIDTH + 4 * ML_WIDTH, 2 * RG_WIDTH + 4 * ML_WIDTH + ML_HEADS]
    x_rg, g_rg, q, k, v, o, i_pre, f_pre = jnp.split(z, cuts, axis=-1)
    xc = causal_dwconv(x_rg, rg_conv_w, rg_conv_b)
    y_rg = rg_lru(xc, rg_w_a, rg_b_a, rg_w_x, rg_b_x, rg_lambda) * jax.nn.gelu(g_rg.astype(f32), approximate=True)
    qk = jax.nn.silu(causal_dwconv(jnp.concatenate([q, k], axis=-1), ml_conv_w, ml_conv_b))
    q, k = jnp.split(qk, 2, axis=-1)
    hm = mlstm_chunkwise(q.reshape(bsz, s, ML_HEADS, ML_HEAD_DIM), k.reshape(bsz, s, ML_HEADS, ML_HEAD_DIM),
                         v.reshape(bsz, s, ML_HEADS, ML_HEAD_DIM), i_pre, f_pre)
    hm = rms_norm(hm, ml_norm.reshape(ML_HEADS, ML_HEAD_DIM))
    y_ml = jax.nn.sigmoid(o.astype(f32)) * hm.reshape(bsz, s, ML_WIDTH)
    y = jnp.concatenate([y_rg, y_ml], axis=-1).astype(h.dtype)
    return y @ w_out

def rope_tables(positions):
    half = AT_HEAD_DIM // 2
    inv_freq = ROPE_THETA ** (-jnp.arange(half, dtype=jnp.float32) * (2.0 / AT_HEAD_DIM))
    ang = positions.astype(jnp.float32)[..., None] * inv_freq
    return jnp.cos(ang)[:, :, None, :], jnp.sin(ang)[:, :, None, :]

def apply_rope(x, cos, sin):
    xf = x.astype(jnp.float32)
    x1, x2 = jnp.split(xf, 2, axis=-1)
    return jnp.concatenate([x1 * cos - x2 * sin, x2 * cos + x1 * sin], axis=-1)

def banded_sink_attention(q, k, v, sinks):
    f32 = jnp.float32
    bsz, s, _, dh = q.shape
    nb = s // WINDOW
    grp = AT_HEADS // AT_KV_HEADS
    qb = q.astype(f32).reshape(bsz, nb, WINDOW, AT_KV_HEADS, grp, dh)

    def key_window(t):
        tb = t.astype(f32).reshape(bsz, nb, WINDOW, AT_KV_HEADS, dh)
        prev = jnp.pad(tb, ((0, 0), (1, 0), (0, 0), (0, 0), (0, 0)))[:, :-1]
        return jnp.concatenate([prev, tb], axis=2)

    kw = key_window(k)
    vw = key_window(v)
    logits = jnp.einsum('bnqhgd,bnkhd->bnhgqk', qb, kw) * (dh ** -0.5)
    qi = jnp.arange(WINDOW)[:, None]
    kj = jnp.arange(2 * WINDOW)[None, :]
    band = (kj > qi) & (kj <= qi + WINDOW)
    blk = jnp.arange(nb)[:, None, None]
    valid = band[None] & ((blk > 0) | (kj >= WINDOW)[None])
    logits = jnp.where(valid[None, :, None, None], logits, -jnp.inf)
    sink = sinks.astype(f32).reshape(AT_KV_HEADS, grp)[:, :, None]
    m = jnp.maximum(jnp.max(logits, axis=-1), sink)
    probs = jnp.exp(logits - m[..., None])
    denom = jnp.sum(probs, axis=-1) + jnp.exp(sink - m)
    out = jnp.einsum('bnhgqk,bnkhd->bnhgqd', probs, vw) / denom[..., None]
    return out.transpose(0, 1, 4, 2, 3, 5).reshape(bsz, s, AT_HEADS * dh)

def swa_sink_mixer(h, positions, w_qkv, q_norm, k_norm, sinks, w_out):
    bsz, s, _ = h.shape
    qkv = h @ w_qkv
    q, k, v = jnp.split(qkv, [AT_HEADS * AT_HEAD_DIM, (AT_HEADS + AT_KV_HEADS) * AT_HEAD_DIM], axis=-1)
    q = q.reshape(bsz, s, AT_HEADS, AT_HEAD_DIM)
    k = k.reshape(bsz, s, AT_KV_HEADS, AT_HEAD_DIM)
    v = v.reshape(bsz, s, AT_KV_HEADS, AT_HEAD_DIM)
    cos, sin = rope_tables(positions)
    q = apply_rope(rms_norm(q, q_norm), cos, sin)
    k = apply_rope(rms_norm(k, k_norm), cos, sin)
    o = banded_sink_attention(q, k, v, sinks)
    return o.astype(h.dtype) @ w_out

def conv_ffn(h, w_up, conv_w, conv_b, w_down):
    g, u = jnp.split(h @ w_up, 2, axis=-1)
    g = causal_dwconv(g, conv_w, conv_b)
    return (jax.nn.gelu(g, approximate=True) * u) @ w_down

def _normal(key, shape, scale):
    return jax.random.normal(key, shape, jnp.float32) * scale

def second_inputs(seed: int = 0) -> dict:
    key = jax.random.key(seed)
    ks = jax.random.split(key, 30)
    x = _normal(ks[0], (BATCH, SEQ, D_MODEL), 1.0)
    p = _normal(ks[1], (DEPTH_2, BATCH, SEQ, PLE_DIM), 1.0)
    offs = jax.random.randint(ks[2], (BATCH, 1), 0, 1024, dtype=jnp.int32)
    positions = offs + jnp.arange(SEQ, dtype=jnp.int32)[None, :]
    norm_mix = 1.0 + _normal(ks[3], (DEPTH_2, D_MODEL), 0.05)
    norm_ffn = 1.0 + _normal(ks[4], (DEPTH_2, D_MODEL), 0.05)
    norm_ple = 1.0 + _normal(ks[5], (DEPTH_2, D_MODEL), 0.05)
    hy_w_in = _normal(ks[6], (N_EVEN, D_MODEL, HY_IN), D_MODEL ** -0.5)
    hy_b_in = _normal(ks[7], (N_EVEN, HY_IN), 0.02)
    hy_b_in = hy_b_in.at[:, HY_IN - ML_HEADS:].add(jnp.linspace(3.0, 6.0, ML_HEADS))
    rg_conv_w = _normal(ks[8], (N_EVEN, RG_CONV, RG_WIDTH), RG_CONV ** -0.5)
    rg_conv_b = _normal(ks[9], (N_EVEN, RG_WIDTH), 0.02)
    rg_w_a = _normal(ks[10], (N_EVEN, RG_BLOCKS, RG_BLOCK, RG_BLOCK), RG_BLOCK ** -0.5)
    rg_b_a = _normal(ks[11], (N_EVEN, RG_WIDTH), 0.02)
    rg_w_x = _normal(ks[12], (N_EVEN, RG_BLOCKS, RG_BLOCK, RG_BLOCK), RG_BLOCK ** -0.5)
    rg_b_x = _normal(ks[13], (N_EVEN, RG_WIDTH), 0.02)
    a_c = jax.random.uniform(ks[14], (N_EVEN, RG_WIDTH), jnp.float32, 0.9, 0.999)
    a_base = a_c ** (1.0 / RG_C)
    rg_lambda = jnp.log(a_base) - jnp.log1p(-a_base)
    ml_conv_w = _normal(ks[15], (N_EVEN, ML_CONV, 2 * ML_WIDTH), ML_CONV ** -0.5)
    ml_conv_b = _normal(ks[16], (N_EVEN, 2 * ML_WIDTH), 0.02)
    ml_norm = 1.0 + _normal(ks[17], (N_EVEN, ML_WIDTH), 0.05)
    hy_w_out = _normal(ks[18], (N_EVEN, HY_MIX, D_MODEL), HY_MIX ** -0.5)
    at_w_qkv = _normal(ks[19], (N_ODD, D_MODEL, AT_QKV), D_MODEL ** -0.5)
    at_q_norm = 1.0 + _normal(ks[20], (N_ODD, AT_HEAD_DIM), 0.05)
    at_k_norm = 1.0 + _normal(ks[21], (N_ODD, AT_HEAD_DIM), 0.05)
    at_sinks = _normal(ks[22], (N_ODD, AT_HEADS), 0.5)
    at_w_out = _normal(ks[23], (N_ODD, AT_HEADS * AT_HEAD_DIM, D_MODEL), (AT_HEADS * AT_HEAD_DIM) ** -0.5)
    ff_w_up = _normal(ks[24], (DEPTH_2, D_MODEL, 2 * FF_DIM), D_MODEL ** -0.5)
    ff_conv_w = _normal(ks[25], (DEPTH_2, FF_CONV, FF_DIM), FF_CONV ** -0.5)
    ff_conv_b = _normal(ks[26], (DEPTH_2, FF_DIM), 0.02)
    ff_w_down = _normal(ks[27], (DEPTH_2, FF_DIM, D_MODEL), FF_DIM ** -0.5)
    ple_w_gate = _normal(ks[28], (DEPTH_2, D_MODEL, D_MODEL), D_MODEL ** -0.5)
    ple_w_proj = _normal(ks[29], (DEPTH_2, PLE_DIM, D_MODEL), PLE_DIM ** -0.5)
    return {'x': x, 'p': p, 'positions': positions,
            'norm_mix': norm_mix, 'norm_ffn': norm_ffn, 'norm_ple': norm_ple,
            'hy_w_in': hy_w_in, 'hy_b_in': hy_b_in,
            'rg_conv_w': rg_conv_w, 'rg_conv_b': rg_conv_b, 'rg_w_a': rg_w_a, 'rg_b_a': rg_b_a,
            'rg_w_x': rg_w_x, 'rg_b_x': rg_b_x, 'rg_lambda': rg_lambda,
            'ml_conv_w': ml_conv_w, 'ml_conv_b': ml_conv_b, 'ml_norm': ml_norm, 'hy_w_out': hy_w_out,
            'at_w_qkv': at_w_qkv, 'at_q_norm': at_q_norm, 'at_k_norm': at_k_norm, 'at_sinks': at_sinks,
            'at_w_out': at_w_out,
            'ff_w_up': ff_w_up, 'ff_conv_w': ff_conv_w, 'ff_conv_b': ff_conv_b, 'ff_w_down': ff_w_down,
            'ple_w_gate': ple_w_gate, 'ple_w_proj': ple_w_proj}

def second_block(x, p, positions, norm_mix, norm_ffn, norm_ple, hy_w_in, hy_b_in,
              rg_conv_w, rg_conv_b, rg_w_a, rg_b_a, rg_w_x, rg_b_x, rg_lambda,
              ml_conv_w, ml_conv_b, ml_norm, hy_w_out,
              at_w_qkv, at_q_norm, at_k_norm, at_sinks, at_w_out,
              ff_w_up, ff_conv_w, ff_conv_b, ff_w_down, ple_w_gate, ple_w_proj):
    for layer in range(DEPTH_2):
        h = rms_norm(x, norm_mix[layer])
        if layer % 2 == 0:
            e = layer // 2
            mix = rglru_mlstm_mixer(h, hy_w_in[e], hy_b_in[e], rg_conv_w[e], rg_conv_b[e], rg_w_a[e], rg_b_a[e],
                                    rg_w_x[e], rg_b_x[e], rg_lambda[e], ml_conv_w[e], ml_conv_b[e], ml_norm[e],
                                    hy_w_out[e])
        else:
            o = layer // 2
            mix = swa_sink_mixer(h, positions, at_w_qkv[o], at_q_norm[o], at_k_norm[o], at_sinks[o], at_w_out[o])
        x = x + mix.astype(x.dtype)
        x = x + conv_ffn(rms_norm(x, norm_ffn[layer]), ff_w_up[layer], ff_conv_w[layer], ff_conv_b[layer],
                         ff_w_down[layer]).astype(x.dtype)
        gate = jax.nn.sigmoid(rms_norm(x, norm_ple[layer]) @ ple_w_gate[layer])
        x = x + (gate * (p[layer] @ ple_w_proj[layer])).astype(x.dtype)
    return x


def setup_inputs(seed=0):
    out = dict(first_inputs(seed))
    for name, value in second_inputs(seed + 1).items():
        if name != "x":
            out[name + "_2"] = value
    return out


def reference(
    x, meta_tokens, ffn1_pre_g, ffn1_w_gate, ffn1_w_up, ffn1_w_down, ffn1_post_g, mix_pre_g,
    w_in, b_gate, q_norm_g, w_uq, kv_norm_g, w_ukv, w_sb_o, w_mla_o, w_out, mix_post_g,
    ffn2_pre_g, ffn2_w_gate, ffn2_w_up, ffn2_w_down, ffn2_post_g, p_2, positions_2, norm_mix_2,
    norm_ffn_2, norm_ple_2, hy_w_in_2, hy_b_in_2, rg_conv_w_2, rg_conv_b_2, rg_w_a_2, rg_b_a_2,
    rg_w_x_2, rg_b_x_2, rg_lambda_2, ml_conv_w_2, ml_conv_b_2, ml_norm_2, hy_w_out_2,
    at_w_qkv_2, at_q_norm_2, at_k_norm_2, at_sinks_2, at_w_out_2, ff_w_up_2, ff_conv_w_2,
    ff_conv_b_2, ff_w_down_2, ple_w_gate_2, ple_w_proj_2,
):
    x = first_block(
        x, meta_tokens, ffn1_pre_g, ffn1_w_gate, ffn1_w_up, ffn1_w_down, ffn1_post_g, mix_pre_g,
        w_in, b_gate, q_norm_g, w_uq, kv_norm_g, w_ukv, w_sb_o, w_mla_o, w_out, mix_post_g,
        ffn2_pre_g, ffn2_w_gate, ffn2_w_up, ffn2_w_down, ffn2_post_g,
    )
    return second_block(
        x, p_2, positions_2, norm_mix_2, norm_ffn_2, norm_ple_2, hy_w_in_2, hy_b_in_2,
        rg_conv_w_2, rg_conv_b_2, rg_w_a_2, rg_b_a_2, rg_w_x_2, rg_b_x_2, rg_lambda_2,
        ml_conv_w_2, ml_conv_b_2, ml_norm_2, hy_w_out_2, at_w_qkv_2, at_q_norm_2, at_k_norm_2,
        at_sinks_2, at_w_out_2, ff_w_up_2, ff_conv_w_2, ff_conv_b_2, ff_w_down_2, ple_w_gate_2,
        ple_w_proj_2,
    )


_drawn_inputs = setup_inputs


def setup_inputs(seed=0):
    import zlib

    import numpy as np

    out = dict(_drawn_inputs(seed))
    spreads = {}
    factors = {'ffn1_pre_g': 3.188,
     'ffn1_post_g': 4.491,
     'mix_pre_g': 2.776,
     'b_gate': 8.0,
     'q_norm_g': 8.0,
     'kv_norm_g': 8.0,
     'mix_post_g': 3.537,
     'ffn2_pre_g': 5.679,
     'ffn2_post_g': 7.937,
     'norm_ple_2': 171.488,
     'rg_b_a_2': 64.0,
     'rg_b_x_2': 64.0,
     'ml_conv_b_2': 8.0,
     'ml_norm_2': 4.235,
     'at_q_norm_2': 8.0,
     'at_k_norm_2': 8.0,
     'at_sinks_2': 200.0,
     'ff_conv_b_2': 5.878,
     'norm_ffn_2': 3.389,
     'rg_conv_b_2': 4.668}
    for name, (base, spread) in spreads.items():
        noise = np.random.default_rng([zlib.crc32(name.encode()), seed]).standard_normal(out[name].shape)
        drawn = base * np.exp(spread * noise) if base else spread * noise
        out[name] = __import__('jax').numpy.asarray(drawn.astype(out[name].dtype))
    for name, factor in factors.items():
        out[name] = (out[name] * factor).astype(out[name].dtype)
    return out
```

```python
from contextlib import ExitStack
import math

import numpy as np
import concourse.bass as bass
from concourse import mybir

F32 = mybir.dt.float32
F32R = mybir.dt.float32r
ACT = mybir.ActivationFunctionType
ALU = mybir.AluOpType
AX = mybir.AxisListType.X

P = 128
T = 512
META = 16
TK = T + META
D = 1024
DT = D // P
FF1 = 2816
FF1T = FF1 // P
FF2 = 3072
FF2T = FF2 // P
EPS = 1e-6
NEG = -1e30
RING = 4
SLOT = 1024
UPTO = 99

STREAM = [
    ("f1gu", 2 * FF1T, SLOT), ("f1dn", 4 * DT, 768), ("win", 34, SLOT), ("uq", 4, 576), ("ukv", 2, SLOT),
    ("wo", 8, SLOT), ("wout", DT, SLOT), ("f2gu", 2 * FF1T, SLOT), ("f2dn", 4 * DT, 768),
    ("hyif", 1, 64), ("hyin", 24, SLOT), ("hyout", DT, SLOT),
    ("up0", 2 * FF2T, SLOT), ("dn0", 3 * DT, SLOT), ("pp0", 2, SLOT), ("pg0", DT, SLOT),
    ("qkv", 12, SLOT), ("atout", DT, SLOT),
    ("up1", 2 * FF2T, SLOT), ("dn1", 3 * DT, SLOT), ("pp1", 2, SLOT), ("pg1", DT, SLOT),
]
BASE, CHUNK_SIZE = {}, []
for _name, _n, _size in STREAM:
    BASE[_name] = len(CHUNK_SIZE)
    for _c in range(_n):
        CHUNK_SIZE.append(_size if _size != 768 else (768, 768, 640, 640)[_c % 4])
NCHUNKS = {1: BASE['win'], 2: BASE['uq'], 3: BASE['wo'], 4: BASE['wo'], 5: BASE['f2gu'], 30: BASE['wo'], 6: BASE['hyin'], 7: BASE['hyout'], 8: BASE['up0'], 9: BASE['qkv'], 10: BASE['atout'], 11: BASE['up1']}.get(UPTO, len(CHUNK_SIZE))

VEC = [("ffn1_pre", 8), ("ffn1_post", 8), ("mix_pre", 8), ("b_gate", 16), ("q_norm", 3), ("kv_norm", 2),
       ("mix_post", 8), ("ffn2_pre", 8), ("ffn2_post", 8), ("norm_mix0", 8), ("norm_mix1", 8),
       ("norm_ffn0", 8), ("norm_ffn1", 8), ("norm_ple0", 8), ("norm_ple1", 8), ("hy_b", 24), ("b_i", 1),
       ("b_f", 1), ("rg_cw", 16), ("rg_cb", 4), ("rg_ba", 4), ("rg_bx", 4), ("rg_lam", 4), ("ml_cw", 32),
       ("ml_cb", 8), ("ml_norm", 4), ("at_qn", 1), ("at_kn", 1), ("sinks", 16), ("ff_cw0", 72),
       ("ff_cb0", 24), ("ff_cw1", 72), ("ff_cb1", 24)]
VOFF, _o = {}, 0
for _name, _n in VEC:
    VOFF[_name] = _o
    _o += _n
NVEC = _o
CON = [("ident", 128), ("ones", 128), ("tri", 128), ("negones", 128), ("permm", 128), ("permh", 128),
       ("blk64", 128), ("dup0", 128), ("dup1", 128), ("sel", 512), ("band", 256), ("invf", 1)]
COFF, _o = {}, 0
for _name, _n in CON:
    COFF[_name] = _o
    _o += _n
NCON = _o


class Signal:

    def __init__(self, s, base):
        self.s, self.base = s, base

    def __call__(self, n):
        return self.s, n + self.base


def slot_of(base, k, per_body=RING, j=0):
    g = base + k
    return g % RING, g // RING + (per_body // RING) * j, g + per_body * j


def program(nc, d, out):
    with ExitStack() as ctx:
        sems = {}

        def sem(name):
            if name not in sems:
                sems[name] = Signal(ctx.enter_context(nc.semaphore(name)), 0)
            return sems[name]

        ends = {}

        def local(kind, **totals):
            out_ = []
            for i, total in enumerate(totals.values()):
                name = f"{kind}{i}"
                out_.append(Signal(sem(name).s, ends.get(name, 0)))
                ends[name] = ends.get(name, 0) + total
            return out_

        base0 = (nc.sbuf_base + 63) // 64 * 64
        arena = ctx.enter_context(nc.sbuf_tensor("arena", [P, 56800], F32))

        def at(name, off, shape, dt=F32):
            n = 4 * int(np.prod(shape[1:]))
            assert off + n <= 56800 * 4, (name, off, n)
            return nc.alloc_sbuf_tensor_at(name, shape, dt, offset=base0 + off, align_bytes=4)

        o_raw, o_hi, o_lo = 0, 16384, 32768
        o_h = 49152
        o_x = o_h + 4 * DT * TK
        o_big = o_x + 8 * DT * TK
        o_tmp = o_big + 98304
        o_vec = o_tmp + 16896
        o_con = o_vec + 4 * NVEC
        o_end = o_con + 4 * NCON
        assert o_end <= 56800 * 4, o_end
        wraw = at("wraw", o_raw, [P, RING, SLOT])
        whi = at("whi", o_hi, [P, RING, SLOT], F32R)
        wlo = at("wlo", o_lo, [P, RING, SLOT], F32R)
        h = at("h", o_h, [P, DT, TK])
        xh = at("xh", o_x, [P, DT, TK], F32R)
        xl = at("xl", o_x + 4 * DT * TK, [P, DT, TK], F32R)
        f = at("f", o_x + 4 * DT * TK, [P, DT, TK])
        vec = at("vec", o_vec, [P, NVEC])
        con = at("con", o_con, [P, NCON])
        hid1h = at("hid1h", o_big, [P, 2 * FF1T, TK // 2], F32R)
        hid1l = at("hid1l", o_big + 4 * FF1T * TK, [P, 2 * FF1T, TK // 2], F32R)
        hid2h = at("hid2h", o_big, [P, FF2T, T], F32R)
        hid2l = at("hid2l", o_big + 4 * FF2T * T, [P, FF2T, T], F32R)
        sg = at("sg", o_tmp, [P, 4, TK // 2])
        pr = at("pr", o_tmp + 4224, [P, 4, TK // 2])
        gp = at("gp", o_tmp, [P, 2, T + 2])
        gc = at("gc", o_tmp + 4112, [P, 2, T])
        pr2 = at("pr2", o_tmp + 8208, [P, 2, T])
        sq = at("sq", o_tmp + 12672, [P, TK])
        acc = at("acc", o_tmp + 14784, [P, TK])
        ntmp = at("ntmp", o_tmp + 0, [P, 4, TK])
        lnv = at("lnv", o_tmp + 8448, [P, TK])
        rbc = at("rbc", o_tmp + 10560, [P, TK])

        B = o_big
        gates = at("gates", B, [P, 16, T])
        ckv = at("ckv", B + 32768, [P, 6, TK])
        ysbh = at("ysbh", B + 45440, [P, 4, T], F32R)
        ysbl = at("ysbl", B + 53632, [P, 4, T], F32R)
        qs = at("qs", B + 61824, [P, 4, T])
        ks = at("ks", B + 70016, [P, 4, TK])
        vs = at("vs", B + 78464, [P, 5, T])
        X = o_x
        spb = at("spb", X, [P, 2, 4, T])
        spm = at("spm", X + 16384, [META, 2, T])
        ab = at("ab", X + 20480, [P, 2, T])
        eb = at("eb", X + 24576, [P, 2, T])
        at_ = at("aa", X + 28672, [P, 2, T])
        lb = at("lb", B + 88704, [P, 2, T])
        vtmp = at("vtmp", B + 88704, [P, 2, TK])
        cqh = at("cqh", X, [P, 3, TK], F32R)
        cql = at("cql", X + 6336, [P, 3, TK], F32R)
        ckh = at("ckh", X + 12672, [P, 2, TK], F32R)
        ckl = at("ckl", X + 16896, [P, 2, TK], F32R)
        vm = at("vm", X + 21120, [P, 5, 8, 64])
        qm = at("qm", B + 61824, [96, 8, T])
        km = at("km", B + 78208, [96, 8, TK])
        ymh = at("ymh", X, [P, 4, T], F32R)
        yml_ = at("yml_", X + 8192, [P, 4, T], F32R)
        pm = at("pm", o_tmp, [P, 2, TK])
        pT = at("pT", o_tmp + 4224, [P, 2, 640])
        kvf = at("kvf", o_tmp + 9344, [P, 2, TK])
        st = at("st", o_tmp + 13568, [P, 64])
        ropt = at("ropt", B + 95104, [P, TK])
        rrt = at("rrt", X + 31360, [P, 2, 264])
        mixh = at("mixh", B + 61824, [P, DT, T], F32R)
        mixl = at("mixl", B + 78208, [P, DT, T], F32R)
        mt = at("mt", o_tmp, [P, 3, T])

        xrg = at("xrg", B, [P, 4, T + 3])
        qkr = at("qkr", B + 8240, [P, 8, T + 3])
        grg = at("grg", B + 24720, [P, 4, T])
        osg = at("osg", B + 32912, [P, 4, T])
        vml = at("vml", B + 41104, [P, 4, T])
        yh = at("yh", B + 49296, [P, 8, T], F32R)
        yl = at("yl", B + 65680, [P, 8, T], F32R)
        xc = at("xc", B + 82064, [P, 4, T])
        ccol = at("ccol", B + 90384, [P, 4, 4])
        rga = at("rga", X, [P, 4, T])
        rgi = at("rgi", X + 8192, [P, 4, T])
        rgu = at("rgu", X + 16384, [P, 4, T])
        rgt = at("rgt", X + 24576, [P, 4, T])
        rwa = at("rwa", B + 90448, [P, 4, P])
        rwx = at("rwx", B + 92496, [P, 4, P])
        qkc = at("qkc", X, [P, 8, T])
        rows = at("rows", o_tmp, [4, 6, T])
        mst = at("mst", X + 16384, [P, 4, T])
        msw = at("msw", X + 24576, [P, 2, T])
        mnum = at("mnum", B + 82064, [P, 2, T])
        mden = at("mden", B + 86160, [P, T])
        prj = at("prj", B, [P, DT, T])
        ptx = at("ptx", B + 16384, [P, 2, T])
        ph = at("ph", B + 20480, [P, 2, T], F32R)
        pl = at("pl", B + 24576, [P, 2, T], F32R)
        sgp = at("sgp", B + 28672, [P, 2, T])
        qa = at("qa", B, [P, 8, T])
        ka = at("ka", B + 16384, [P, 2, T])
        va = at("va", B + 20480, [P, 4, 256])
        ayh = at("ayh", B + 24576, [P, 8, T], F32R)
        ayl = at("ayl", B + 40960, [P, 8, T], F32R)
        cosr = at("cosr", B + 57344, [P, T])
        sinr = at("sinr", B + 59392, [P, T])
        kdup = at("kdup", B + 61440, [P, 4, T])
        qsq = at("qsq", B + 69632, [P, 2, T])
        qrb = at("qrb", B + 73728, [P, 2, T])
        qt1 = at("qt1", B + 77824, [P, 2, T])
        qt2 = at("qt2", B + 81920, [P, 2, T])
        posb = at("posb", B + 86016, [P, T], mybir.dt.int32)
        ang = at("ang", B + 88064, [P, 3, T])
        asx = at("asx", X, [P, 2, 4, 256])
        apt = at("apt", X + 8192, [P, 2, 1024])
        ast_ = at("ast_", X + 16384, [P, 2, 8, 4])
        vta = at("vta", X + 16896, [P, 2, T])

        PS = ctx.enter_context(nc.psum_tensor("PS", [P, 8 * 512], F32))
        PS3 = PS[:, :].rearrange("p (b n) -> p b n", b=8)

        def bank(b, n=1, w=512, rows=P):
            return PS3[0:rows, b:b + n, 0:w]

        def c_(name, lo=0, hi=None, rows=slice(0, P)):
            return con[rows, COFF[name] + lo:COFF[name] + (dict(CON)[name] if hi is None else hi)]

        def v_(name, t=0):
            return vec[:, VOFF[name] + t:VOFF[name] + t + 1]

        raw_landed = [sem(f"raw_landed{s}") for s in range(RING)]
        hi_done = sem("hi_done")
        lo_done = sem("lo_done")
        chunk_used = sem("chunk_used")

        def load(sp, base, k, per_body=RING, j=0):
            s, rnd, g = slot_of(base, k, per_body, j)
            size = CHUNK_SIZE[base + k]
            if base + k >= RING:
                sp.wait_ge(*lo_done(g - (RING - 1)))
            return s, size

        def split_hi(act, base, k, per_body=RING, j=0):
            if base + k >= NCHUNKS:
                return
            s, rnd, g = slot_of(base, k, per_body, j)
            size = CHUNK_SIZE[base + k]
            act.wait_ge(*raw_landed[s]((rnd + 1) * 16))
            if base + k >= RING:
                act.wait_ge(*chunk_used(g - (RING - 1)))
            act.activation(whi[:, s, 0:size], wraw[:, s, 0:size], ACT.Copy).then_inc(hi_done.s, 1)

        def split_lo(pool, base, k, per_body=RING, j=0):
            s, rnd, g = slot_of(base, k, per_body, j)
            size = CHUNK_SIZE[base + k]
            pool.wait_ge(*hi_done(g + 1))
            pool.tensor_tensor(wlo[:, s, 0:size], wraw[:, s, 0:size], whi[:, s, 0:size].bitcast(F32),
                               ALU.subtract).then_inc(lo_done.s, 1)

        def mm3(pe, out_, s, a, b, xhi, xlo, start, stop):
            pe.matmul(out_, whi[:, s, a:b], xhi, start=start, stop=False, skip_group_check=True)
            pe.matmul(out_, whi[:, s, a:b], xlo, start=False, stop=False, skip_group_check=True)
            return pe.matmul(out_, wlo[:, s, a:b], xhi, start=False, stop=stop, skip_group_check=True)

        bars = {"pe": 0, "act": 0, "dve": 0}
        phase_over = sem("phase_over")

        def phase_end(eng, who):
            bars[who] += 1
            eng.drain().then_inc(phase_over.s, 1)
            eng.wait_ge(*phase_over(3 * bars[who]))

        links = {}

        class Chain:
            def __init__(self, eng, name):
                self.eng, self.sig = eng, sem(name)

            def link(self, ins):
                links[self.sig] = links.get(self.sig, 0) + 1
                ins.then_inc(self.sig.s, 1)
                self.eng.wait_ge(*self.sig(links[self.sig]))

        def weights(name):
            base, n = BASE[name], dict((a, b) for a, b, _ in STREAM)[name]
            src = d["w_" + name]
            assert ahead_base[0] == base
            ahead_base[0] = base + n
            size = {a: c for a, _, c in STREAM}[name]

            def where(k, j):
                if size == 768:
                    off = (0, 768, 1536, 2176)[k % 4]
                    return src[bass.ds(j + k // 4, 1), :, off:off + CHUNK_SIZE[base + k]]
                return src[bass.ds(j * RING + k, 1), :, :]

            def one(sp, k, j):
                s, size_ = load(sp, base, k, RING, j)
                sp.dma_start(wraw[:, s, 0:size_], where(k, j).rearrange("a p n -> p (a n)")).then_inc(raw_landed[s].s, 16)

            def sp_(sp):
                first = 0
                if base < RING:
                    for k in range(RING):
                        one(sp, k, 0)
                    first = 1
                if n % RING == 0 and n // RING - first > 1:
                    with sp.Fori(first, n // RING) as j:
                        for k in range(RING):
                            s, rnd, g = slot_of(base, k, RING, j)
                            sp.wait_ge(*lo_done(g - (RING - 1)))
                            sz = CHUNK_SIZE[base + k]
                            sp.dma_start(wraw[:, s, 0:sz], where(k, j).rearrange("a p n -> p (a n)")).then_inc(raw_landed[s].s, 16)
                else:
                    for k in range(first * RING, n):
                        one(sp, k, 0)

            def pool_(pool):
                k0 = max(0, low_until[0] - base)
                low_until[0] = max(low_until[0], base + n)
                if n % RING == 0 and n // RING > 1:
                    start = -(-k0 // RING)
                    for k in range(k0, start * RING):
                        split_lo(pool, base, k)
                    with pool.Fori(start, n // RING) as j:
                        for k in range(RING):
                            split_lo(pool, base, k, RING, j)
                else:
                    for k in range(k0, n):
                        split_lo(pool, base, k)
            return sp_, pool_

        low_until = [0]

        def split_ahead(pool, base):
            while low_until[0] < min(base + RING, NCHUNKS):
                split_lo(pool, 0, low_until[0])
                low_until[0] += 1

        PE, AC, DV, PO, SP = [], [], [], [], []
        ahead_base = [0]

        def stage(pe=None, act=None, dve=None, pool=None, sp=None):
            if pe: PE.append(pe)
            if act: AC.append(act)
            if dve: DV.append(dve)
            if pool: PO.append(pool)
            if sp: SP.append(sp)

        in_landed = sem("in_landed")

        xn_done = {}

        def s_load():
            def sp(sp):
                for t in range(DT):
                    sp.dma_start(h[:, t, :], d["xT"][t]).then_inc(sem(f"x_landed{t}").s, 16)
                sp.dma_start(vec[:, :], d["vec"]).then_inc(in_landed.s, 16)
                sp.dma_start(con[:, :], d["con"]).then_inc(in_landed.s, 16)

            def act(act):
                act.preload_act_table_set("natural_log_exp_and_others")
                for t in range(DT):
                    act.wait_ge(*sem(f"x_landed{t}")(16))
                    if t >= 2:
                        act.wait_ge(*sem("sq0_added")(t - 1))
                    act.activation(pr3(t % 2), h[:, t, :], ACT.Square).then_inc(sem("sq0").s, 1)
                for k in range(RING):
                    split_hi(act, 0, k)

            def dve(dve):
                for t in range(DT):
                    dve.wait_ge(*sem("sq0")(t + 1))
                    if t == 0:
                        dve.tensor_copy(acc[:, :], pr3(0)).then_inc(sem("sq0_added").s, 1)
                    else:
                        dve.wait_ge(*sem("sq0_added")(t))
                        dve.tensor_tensor(acc[:, :], acc[:, :], pr3(t % 2), ALU.add).then_inc(sem("sq0_added").s, 1)
                dve.wait_ge(*in_landed(32))

            def pe(pe):
                pe.wait_ge(*in_landed(32))
            stage(pe, act, dve, None, sp)

        def pr3(i):
            return ntmp[:, i, :]

        def rsq(sums, n, k):
            acc_whole, sum_done, ln_done, rbc_done = sums
            H = 2 if n == TK else 1
            w = n // H

            def pe(pe):
                pe.wait_ge(*acc_whole(1))
                for i in range(H):
                    ins = pe.matmul(PS3[:, 6 + i, 0:w], c_("ones"), acc[:, i * w:(i + 1) * w], start=True, stop=True)
                ins.then_inc(sum_done.s, 1)

            def act(act):
                act.wait_ge(*sum_done(1))
                act.activation(lnv[:, 0:n].rearrange("p (a q) -> p a q", a=H), bank(6, H, w), ACT.Ln,
                               bias=epsc[:, 0:1], scale=1.0 / k).then_inc(ln_done.s, 1)
                act.wait_ge(*ln_done(1))
                act.activation(rbc[:, 0:n], lnv[:, 0:n], ACT.Exp, scale=-0.5).then_inc(rbc_done.s, 1)
            return pe, act

        epsc = at("epsc", o_end, [P, 4])

        def s_prenorm(tag, gain, n, k=D, tiles=DT, src=None, dst=None, meet=True, early=(None, None), sums_there=None):
            src = h if src is None else src
            dh, dl = (xh, xl) if dst is None else dst
            acc_whole, sum_done, ln_done, rbc_done, n_done, nh_done, even, odd = local(
                "norm", acc=1, sum=1, ln=1, rbc=1, normed=tiles, high=tiles, even=(tiles + 1) // 2, odd=tiles // 2)
            xn_done[tag] = even, odd
            pe_, act_ = rsq((acc_whole, sum_done, ln_done, rbc_done), n, k)

            def low(eng, t):
                eng.wait_ge(*nh_done(t + 1))
                eng.tensor_tensor(dl[:, t, 0:n], ntmp[:, t % 4, 0:n], dh[:, t, 0:n].bitcast(F32),
                                  ALU.subtract).then_inc(xn_done[tag][t % 2].s, 1)

            def pe(pe):
                if meet:
                    phase_end(pe, "pe")
                pe_(pe)

            def act(act):
                if meet:
                    phase_end(act, "act")
                if early[0]:
                    early[0](act)
                act.preload_act_table_set("natural_log_exp_and_others")
                act_(act)
                for t in range(tiles):
                    act.wait_ge(*n_done(t + 1))
                    act.activation(dh[:, t, 0:n], ntmp[:, t % 4, 0:n], ACT.Copy).then_inc(nh_done.s, 1)

            def dve(dve):
                if meet:
                    phase_end(dve, "dve")
                dve.sem_inc(acc_whole.s, 1)
                if early[1]:
                    early[1](dve)
                dve.wait_ge(*rbc_done(1))
                for t in range(tiles):
                    if t >= 4:
                        dve.wait_ge(*xn_done[tag][t % 2](t // 2 - 1))
                    dve.scalar_tensor_tensor(ntmp[:, t % 4, 0:n], src[:, t, 0:n], v_(gain, t), rbc[:, 0:n],
                                             ALU.mult, ALU.mult).then_inc(n_done.s, 1)
                    if t >= 1 and (t % 2 or tiles < DT):
                        low(dve, t - 1)
                if tiles < DT:
                    low(dve, tiles - 1)

            base = ahead_base[0]

            def pool(pool):
                split_ahead(pool, base)
                for t in range(1, tiles, 2):
                    low(pool, t)
            stage(pe, act, dve, pool if tiles == DT else None)

        def xn_ready(pe, tag, t):
            pe.wait_ge(*xn_done[tag][t % 2](t // 2 + 1))

        def s_postnorm(tag, gain, n, factor):
            acc_whole, sum_done, ln_done, rbc_done, h_done, added, squared, scaled = local(
                "post", acc=1, sum=1, ln=1, rbc=1, h=DT, added=DT, sq=DT, scaled=DT)
            pe_, act_ = rsq((acc_whole, sum_done, ln_done, rbc_done), n, D)

            def pe(pe):
                phase_end(pe, "pe")
                pe_(pe)

            def act(act):
                phase_end(act, "act")
                act.preload_act_table_set("natural_log_exp_and_others")
                act_(act)
                for t in range(DT):
                    act.wait_ge(*h_done(t + 1))
                    if t >= 2:
                        act.wait_ge(*added(t - 1))
                    act.activation(ntmp[:, 2 + t % 2, 0:n], h[:, t, 0:n], ACT.Square).then_inc(squared.s, 1)

            def dve(dve):
                phase_end(dve, "dve")
                dve.sem_inc(acc_whole.s, 1)
                dve.wait_ge(*rbc_done(1))

                def add(t):
                    dve.wait_ge(*squared(t + 1))
                    if t == 0:
                        dve.tensor_copy(acc[:, 0:n], ntmp[:, 2, 0:n]).then_inc(added.s, 1)
                    else:
                        dve.wait_ge(*added(t))
                        dve.tensor_tensor(acc[:, 0:n], acc[:, 0:n], ntmp[:, 2 + t % 2, 0:n],
                                          ALU.add).then_inc(added.s, 1)
                for t in range(DT):
                    if t >= 2:
                        dve.wait_ge(*h_done(t - 1))
                    dve.scalar_tensor_tensor(ntmp[:, t % 2, 0:n], f[:, t, 0:n], v_(gain, t), rbc[:, 0:n],
                                             ALU.mult, ALU.mult).then_inc(scaled.s, 1)
                    dve.wait_ge(*scaled(t + 1))
                    dve.scalar_tensor_tensor(h[:, t, 0:n], ntmp[:, t % 2, 0:n], factor, h[:, t, 0:n],
                                             ALU.mult, ALU.add).then_inc(h_done.s, 1)
                    if t >= 1:
                        add(t - 1)
                add(DT - 1)
            stage(pe, act, dve)

        def s_gate_up(name, xn, n):
            base = BASE[name]
            H = 2 if n == TK else 1
            w = n // H
            turns = FF1T // 2
            dh, dl = (hid1h, hid1l) if H == 2 else (hid2h, hid2l)
            g_act, u_free, own = local("up", g_act=1 + turns, u_free=1 + turns, own=2 * turns)
            sga = at(name + "sg", o_tmp, [P, 2 * H, w])
            pra = at(name + "pr", o_tmp + 4224, [P, 2 * H, w])

            def pe(pe):
                def turn(j, first):
                    for k in range(4):
                        s, _, g = slot_of(base, k, 4, j)
                        if k == 0 and not first:
                            pe.wait_ge(*g_act(j + 1))
                        if k == 2 and not first:
                            pe.wait_ge(*u_free(j + 1))
                        pe.wait_ge(*lo_done(g + 1))
                        for i in range(H):
                            o = PS3[:, H * k + i, 0:w]
                            for kt in range(DT):
                                if first and k == 0 and i == 0:
                                    xn_ready(pe, xn, kt)
                                ins = mm3(pe, o, s, kt * P, (kt + 1) * P, xh[:, kt, i * w:(i + 1) * w],
                                          xl[:, kt, i * w:(i + 1) * w], kt == 0, kt == DT - 1)
                        ins.then_inc(chunk_used.s, 1)
                turn(0, True)
                with pe.Fori(1, turns) as j:
                    turn(j, False)

            def turn_act(act, j, ahead):
                ahead(act, 0)
                ahead(act, 1)
                act.wait_ge(*u_free(j + 1))
                act.activation(sga[:, :, :], bank(0, 2 * H, w), ACT.Silu).then_inc(g_act.s, 1)
                ahead(act, 2)
                ahead(act, 3)

            def act(act):
                act.preload_act_table_set("silu_and_others")
                act.sem_inc(g_act.s, 1)
                with act.Fori(0, turns - 1) as j:
                    turn_act(act, j, lambda a, k: split_hi(a, base, 4 + k, 4, j))
                turn_act(act, turns - 1, lambda a, k: split_hi(a, base, 4 * turns + k))

            def dve(dve):
                dve.sem_inc(u_free.s, 1)
                with dve.Fori(0, turns) as j:
                    dve.wait_ge(*chunk_used(base + 4 + 4 * j))
                    dve.wait_ge(*g_act(j + 2))
                    dst = slice(None), bass.ds(2 * H * j, 2 * H), slice(None)
                    dve.tensor_tensor(pra[:, :, :], sga[:, :, :], bank(2 * H, 2 * H, w), ALU.mult).then_inc(own.s, 1)
                    dve.tensor_tensor(dh[dst], sga[:, :, :], bank(2 * H, 2 * H, w), ALU.mult).then_inc(u_free.s, 1)
                    dve.wait_ge(*own(2 * j + 1))
                    dve.wait_ge(*u_free(j + 2))
                    dve.tensor_tensor(dl[dst], pra[:, :, :], dh[dst].bitcast(F32), ALU.subtract).then_inc(own.s, 1)
                    dve.wait_ge(*own(2 * j + 2))
            sp_, pool_ = weights(name)

            stage(pe, act, dve, pool_, sp_)

        def s_conv_up(name, xn, layer):
            base = BASE[name]
            turns = FF2T // 2
            cw, cb = VOFF[f"ff_cw{layer}"], VOFF[f"ff_cb{layer}"]
            g_read, u_free, own, conv, gel = local(
                "up", g_read=1 + turns, u_free=1 + turns, own=6 * turns, conv=1 + turns, gelu=turns)

            def pe(pe):
                def turn(j, first):
                    for k in range(4):
                        s, _, g = slot_of(base, k, 4, j)
                        if k == 0 and not first:
                            pe.wait_ge(*g_read(j + 1))
                        if k == 2 and not first:
                            pe.wait_ge(*u_free(j + 1))
                        pe.wait_ge(*lo_done(g + 1))
                        for kt in range(DT):
                            if first and k == 0:
                                xn_ready(pe, xn, kt)
                            ins = mm3(pe, PS3[:, k, :], s, kt * P, (kt + 1) * P, xh[:, kt, 0:T], xl[:, kt, 0:T],
                                      kt == 0, kt == DT - 1)
                        ins.then_inc(chunk_used.s, 1)
                turn(0, True)
                with pe.Fori(1, turns) as j:
                    turn(j, False)

            def turn_act(act, j, ahead):
                ahead(act, 0)
                ahead(act, 1)
                act.wait_ge(*conv(j + 1))
                act.activation(gp[:, :, 2:T + 2], bank(0, 2), ACT.Copy).then_inc(g_read.s, 1)
                ahead(act, 2)
                act.wait_ge(*conv(j + 2))
                act.activation(gc[:, :, :], gc[:, :, :], ACT.Gelu_apprx_tanh).then_inc(gel.s, 1)
                ahead(act, 3)

            def act(act):
                act.preload_act_table_set("gelu_apprx_tanh_and_others")
                act.sem_inc(g_read.s, 1)
                with act.Fori(0, turns - 1) as j:
                    turn_act(act, j, lambda a, k: split_hi(a, base, 4 + k, 4, j))
                turn_act(act, turns - 1, lambda a, k: split_hi(a, base, 4 * turns + k))

            def dve(dve):
                dve.memset(gp[:, :, 0:2], 0.0).then_inc(conv.s, 1)
                dve.sem_inc(u_free.s, 1)
                with dve.Fori(0, turns) as j:
                    dve.wait_ge(*g_read(j + 2))
                    for m in range(2):
                        dve.tensor_scalar(gc[:, m, :], gp[:, m, 0:T], vec[:, bass.ds(2 * j + (cw + m), 1)],
                                          vec[:, bass.ds(2 * j + (cb + m), 1)], ALU.mult, ALU.add).then_inc(own.s, 1)
                    for tap in (1, 2):
                        for m in range(2):
                            dve.wait_ge(*own(6 * j + (2 * tap - 1 + m)))
                            ins = dve.scalar_tensor_tensor(
                                gc[:, m, :], gp[:, m, tap:T + tap], vec[:, bass.ds(2 * j + (cw + FF2T * tap + m), 1)],
                                gc[:, m, :], ALU.mult, ALU.add)
                            if tap == 1:
                                ins.then_inc(own.s, 1)
                            elif m == 1:
                                ins.then_inc(conv.s, 1)
                    dve.wait_ge(*chunk_used(base + 4 + 4 * j))
                    dve.wait_ge(*gel(j + 1))
                    dst = slice(None), bass.ds(2 * j, 2), slice(None)
                    dve.tensor_tensor(pr2[:, :, :], gc[:, :, :], bank(2, 2), ALU.mult).then_inc(own.s, 1)
                    dve.tensor_tensor(hid2h[dst], gc[:, :, :], bank(2, 2), ALU.mult).then_inc(u_free.s, 1)
                    dve.wait_ge(*own(6 * j + 5))
                    dve.wait_ge(*u_free(j + 2))
                    dve.tensor_tensor(hid2l[dst], pr2[:, :, :], hid2h[dst].bitcast(F32),
                                      ALU.subtract).then_inc(own.s, 1)
                    dve.wait_ge(*own(6 * j + 6))
            sp_, pool_ = weights(name)
            stage(pe, act, dve, pool_, sp_)

        def s_out(name, kts, rhs, n, tiles_per_turn, residual, wait=None):
            base = BASE[name]
            H = 2 if n == TK else 1
            w = n // H
            lens = kts
            per_body = tiles_per_turn * len(kts)
            turns = DT // tiles_per_turn
            free, own = local("out", free=2 + DT, own=1 + 2 * DT)
            hv = (h if residual else f)
            dst_t = hv[:, :, :].rearrange("p t (a q) -> p (t a) q", a=2)

            def dst(t):
                if H == 2:
                    return dst_t[:, bass.ds(2 * t, 2), :]
                return hv[:, bass.ds(t, 1), 0:T]
            sq3 = sq[:, 0:n].rearrange("p (a q) -> p a q", a=H)
            acc3 = acc[:, 0:n].rearrange("p (a q) -> p a q", a=H)

            def pe(pe):
                phase_end(pe, "pe")
                if wait:
                    pe.wait_ge(*wait)
                with pe.Fori(0, turns) as j:
                    for u in range(tiles_per_turn):
                        b = H * (u % 2)
                        pe.wait_ge(*free(tiles_per_turn * j + (u + 1)))
                        kt = 0
                        for c, nk in enumerate(lens):
                            s, _, g = slot_of(base, u * len(lens) + c, per_body, j)
                            pe.wait_ge(*lo_done(g + 1))
                            for i in range(H):
                                for q in range(nk):
                                    yh_, yl_ = rhs(kt + q, i)
                                    ins = mm3(pe, PS3[:, b + i, 0:w], s, q * P, (q + 1) * P, yh_, yl_,
                                              kt + q == 0, kt + q == sum(lens) - 1)
                            ins.then_inc(chunk_used.s, 1)
                            kt += nk

            def act(act):
                phase_end(act, "act")

                def turn(j, ahead):
                    for k in range(per_body):
                        ahead(k)
                if turns > 1:
                    with act.Fori(0, turns - 1) as j:
                        turn(j, lambda k: split_hi(act, base, 4 + k, per_body, j))
                turn(turns - 1, lambda k: split_hi(act, base, per_body * (turns - 1) + 4 + k))

            def dve(dve):
                phase_end(dve, "dve")
                dve.memset(acc[:, 0:n], 0.0).then_inc(own.s, 1)
                dve.sem_inc(free.s, 2)
                nl = len(lens)
                with dve.Fori(0, turns) as j:
                    for u in range(tiles_per_turn):
                        t = tiles_per_turn * j + u
                        b = H * (u % 2)
                        dve.wait_ge(*chunk_used(per_body * j + (base + nl * (u + 1))))
                        dve.wait_ge(*own(2 * tiles_per_turn * j + (2 * u + 1)))
                        if residual:
                            dve.tensor_tensor(dst(t), bank(b, H, w), dst(t), ALU.add).then_inc(free.s, 1)
                        else:
                            dve.tensor_scalar(dst(t), bank(b, H, w), 1.0, None, ALU.mult).then_inc(free.s, 1)
                        dve.wait_ge(*free(tiles_per_turn * j + (u + 3)))
                        dve.tensor_tensor(sq3, dst(t), dst(t), ALU.mult).then_inc(own.s, 1)
                        dve.wait_ge(*own(2 * tiles_per_turn * j + (2 * u + 2)))
                        dve.tensor_tensor(acc3, acc3, sq3, ALU.add).then_inc(own.s, 1)
                dve.wait_ge(*own(2 * DT + 1))
            sp_, pool_ = weights(name)
            stage(pe, act, dve, pool_, sp_)

        def rhs_hid(n):
            if n == TK:
                return lambda kt, i: (hid1h[:, 2 * kt + i, :], hid1l[:, 2 * kt + i, :])
            return lambda kt, i: (hid2h[:, kt, :], hid2l[:, kt, :])

        def project(name, xn, n_of, evac, tail=None, first=0, count=None, hooks=None, dve_=None, after=None):
            base = BASE[name]
            count = dict((a, b) for a, b, _ in STREAM)[name] if count is None else count
            read, = local("read", read=count)
            tile_read[name] = read

            def pe(pe):
                for c in range(count):
                    s, _, g = slot_of(base, c)
                    n = n_of(c)
                    H, w = (2, n // 2) if n == TK else (1, n)
                    if c >= 3:
                        pe.wait_ge(*read(c - 2))
                    pe.wait_ge(*lo_done(g + 1))
                    for i in range(H):
                        for kt in range(DT):
                            if c == 0 and i == 0:
                                xn_ready(pe, xn, kt)
                            ins = mm3(pe, PS3[:, 2 * (c % 3) + i, 0:w], s, kt * P, (kt + 1) * P,
                                      xh[:, kt, i * w:(i + 1) * w], xl[:, kt, i * w:(i + 1) * w], kt == 0, kt == DT - 1)
                    ins.then_inc(chunk_used.s, 1)
                    if hooks:
                        hooks(pe, c)
                if hooks:
                    hooks(pe, count)

            def act(act):
                for c in range(count):
                    n = n_of(c)
                    H, w = (2, n // 2) if n == TK else (1, n)
                    act.wait_ge(*chunk_used(base + c + 1))
                    evac(act, c, bank(2 * (c % 3), H, w)).then_inc(read.s, 1)
                    split_hi(act, base, c + 4)
                    if after:
                        after(act, c)
            sp_, pool_ = weights(name)
            stage(pe, act, dve_, pool_, sp_)

        tile_read = {}

        def halves(ap, n):
            return ap.rearrange("p (a q) -> p a q", a=2 if n == TK else 1)

        def s_win():
            def n_of(c):
                return T if c < 4 or c >= 18 else TK
            v_turned, v_kept = local("st", turned=4, kept=4)

            def evac(act, c, ps):
                if c < 4:
                    return act.activation(halves(qs[:, c, :], T), ps, ACT.Copy, scale=0.125)
                if c < 8:
                    return act.activation(halves(ks[:, c - 4, :], TK), ps, ACT.Copy)
                if c < 12:
                    if c >= 10:
                        act.wait_ge(*v_turned(c - 9))
                    return act.activation(halves(vtmp[:, c % 2, :], TK), ps, ACT.Copy)
                if c < 18:
                    return act.activation(halves(ckv[:, c - 12, :], TK), ps, ACT.Copy)
                if c == 18:
                    act.preload_act_table_set("sigmoid_and_others")
                return act.activation(halves(gates[:, c - 18, :], T), ps, ACT.Sigmoid, bias=v_("b_gate", c - 18))

            def hooks(pe, c):
                if 9 <= c < 13:
                    t = c - 9
                    pe.wait_ge(*tile_read["win"](8 + t + 1))
                    if t >= 1:
                        pe.wait_ge(*v_kept(t))
                    for i in range(4):
                        pe.transpose(PS3[:, 6, i * P:(i + 1) * P], vtmp[:, t % 2, i * P:(i + 1) * P], c_("ident"))
                    pe.transpose(PS3[0:META, 7, 0:P], vtmp[:, t % 2, T:TK], c_("ident")).then_inc(v_turned.s, 1)

            def dve(dve):
                for t in range(4):
                    dve.wait_ge(*v_turned(t + 1))
                    dve.tensor_copy(vs[:, 0:4, t * P:(t + 1) * P], PS3[:, 6, :].rearrange("p (i n) -> p i n", i=4))
                    dve.tensor_copy(vs[0:META, 4, t * P:(t + 1) * P], PS3[0:META, 7, 0:P]).then_inc(v_kept.s, 1)
            project("win", "n2", n_of, evac, hooks=hooks, dve_=dve)

        def s_stick():
            HEADS = 8
            units = [(hd, j) for hd in range(HEADS) for j in (3, 2, 1, 0, 4)]
            NU = len(units)

            def first(j):
                return P * j if j < 4 else 0
            z_done, ab_done, e_done, l_done, sp_done, arg_done, a_done, pv_done = local(
                "st", z=NU, ab=NU, e=NU, l=NU, sp=NU, arg=NU, a=NU, pv=NU)
            sp_cut, a_cut, y_hi, y_lo = local("su", spcut=32, acut=32, yhi=4, ylo=4)

            def cut(u):
                return sum(1 for x in units[:u + 1] if x[1] < 4)

            def rows(u):
                return P if units[u][1] < 4 else META

            def spt(u):
                hd, j = units[u]
                return spb[:, hd % 2, j, first(j):T] if j < 4 else spm[:, hd % 2, :]

            def zb(u):
                return PS3[0:rows(u), u % 6, first(units[u][1]):T]

            def pe(pe):
                phase_end(pe, "pe")

                def z(u):
                    hd, j = units[u]
                    r, t, c0 = 64 * (hd % 2), hd // 2, first(j)
                    if u >= 6:
                        pe.wait_ge(*a_done(u - 5))
                    k0, k1 = (c0, c0 + P) if j < 4 else (T, TK)
                    pe.matmul(zb(u), ks[r:r + 64, t, k0:k1], qs[r:r + 64, t, c0:T], start=True, stop=False,
                              skip_group_check=True).then_inc(z_done.s, 1)

                def sums(u):
                    hd, j = units[u]
                    m = rows(u)
                    pe.wait_ge(*sp_done(u + 1))
                    pe.wait_ge(*sp_cut(cut(u)))
                    later = [x for x in range(4) if j == 4 or x > j]
                    for x in later:
                        pe.matmul(PS3[0:m, u % 6, P * x:T], c_("negones", 0, m), spb[:, hd % 2, x, P * x:T],
                                  start=False, stop=False, skip_group_check=True)
                    pe.matmul(zb(u), c_("tri", 0, m, slice(0, m)), spt(u), start=False, stop=True,
                              skip_group_check=True).then_inc(arg_done.s, 1)

                def pv(u):
                    hd, j = units[u]
                    c0, m, r = first(j), rows(u), 64 * (hd % 2)
                    if j < 4:
                        pe.wait_ge(*a_cut(cut(u)))
                    else:
                        pe.wait_ge(*a_done(u + 1))
                    if hd >= 4 and hd % 2 == 0 and j == 3:
                        pe.wait_ge(*y_lo(hd // 2 - 1))
                        pe.wait_ge(*y_hi(hd // 2 - 1))
                    pe.matmul(PS3[r:r + 64, 6 + (hd // 2) % 2, c0:T], vs[0:m, j, hd * 64:(hd + 1) * 64],
                              at_[0:m, u % 2, c0:T], start=(j == 3), stop=(j == 4),
                              skip_group_check=True).then_inc(pv_done.s, 1)
                z(0)
                z(1)
                for u in range(NU):
                    if u + 2 < NU:
                        z(u + 2)
                    sums(u)
                    if u >= 1:
                        pv(u - 1)
                pv(NU - 1)

            def dve(dve):
                phase_end(dve, "dve")

                def sp(u):
                    hd, j = units[u]
                    w = T - first(j)
                    dve.wait_ge(*l_done(u + 1))
                    if hd >= 2:
                        dve.wait_ge(*arg_done(5 * (hd - 1)))
                    dve.scalar_tensor_tensor(spt(u), zb(u), 0.0, lb[0:rows(u), u % 2, 0:w], ALU.max,
                                             ALU.add).then_inc(sp_done.s, 1)

                def y_out(pair):
                    dve.wait_ge(*y_hi(pair + 1))
                    dve.tensor_tensor(ysbl[:, pair, :], PS3[:, 6 + pair % 2, :], ysbh[:, pair, :].bitcast(F32),
                                      ALU.subtract).then_inc(y_lo.s, 1)
                for u in range(NU):
                    sp(u)
                    if u % 10 == 4 and u >= 10:
                        y_out(u // 10 - 1)
                y_out(3)

            def act(act):
                phase_end(act, "act")
                act.preload_act_table_set("natural_log_exp_and_others")

                def e(u):
                    w = T - first(units[u][1])
                    act.wait_ge(*z_done(u + 1))
                    if u >= 2:
                        act.wait_ge(*l_done(u - 1))
                    act.activation(ab[0:rows(u), u % 2, 0:w], zb(u), ACT.Abs).then_inc(ab_done.s, 1)
                    act.wait_ge(*ab_done(u + 1))
                    act.activation(eb[0:rows(u), u % 2, 0:w], ab[0:rows(u), u % 2, 0:w], ACT.Exp,
                                   scale=-1.0).then_inc(e_done.s, 1)
                    act.wait_ge(*e_done(u + 1))
                    if u >= 2:
                        act.wait_ge(*sp_done(u - 1))
                    act.activation(lb[0:rows(u), u % 2, 0:w], eb[0:rows(u), u % 2, 0:w], ACT.Ln,
                                   bias=1.0).then_inc(l_done.s, 1)

                def a(u):
                    act.wait_ge(*arg_done(u + 1))
                    if u >= 2:
                        act.wait_ge(*pv_done(u - 1))
                    act.activation(at_[0:rows(u), u % 2, first(units[u][1]):T], zb(u), ACT.Exp).then_inc(a_done.s, 1)

                def y_out(pair):
                    act.wait_ge(*pv_done(10 * pair + 10))
                    act.activation(ysbh[:, pair, :], PS3[:, 6 + pair % 2, :], ACT.Copy).then_inc(y_hi.s, 1)
                e(0)
                for u in range(NU):
                    if u + 1 < NU:
                        e(u + 1)
                    a(u)
                    if u % 10 == 2 and u >= 10:
                        y_out(u // 10 - 1)
                y_out(3)

            def pool(pool):
                def cut_sp(u):
                    hd, j = units[u]
                    if j == 4:
                        return
                    pool.wait_ge(*sp_done(u + 1))
                    b = spb[:, hd % 2, j, P * j:P * (j + 1)]
                    pool.affine_select(out=b, in_=b, pattern=[[1, P]], compare_op=ALU.is_gt, fill=0.0, base=0,
                                       channel_multiplier=-1).then_inc(sp_cut.s, 1)

                def cut_a(u):
                    hd, j = units[u]
                    if j == 4:
                        return
                    pool.wait_ge(*a_done(u + 1))
                    b = at_[:, u % 2, P * j:P * (j + 1)]
                    pool.affine_select(out=b, in_=b, pattern=[[1, P]], compare_op=ALU.is_gt, fill=0.0, base=0,
                                       channel_multiplier=-1).then_inc(a_cut.s, 1)
                cut_sp(0)
                for u in range(NU):
                    if u + 1 < NU:
                        cut_sp(u + 1)
                    cut_a(u)
            stage(pe, act, dve, pool)

        def s_small_squares(tag, src, t0, tiles, n):
            added, squared = local("small", added=tiles, sq=tiles)

            def act(act):
                for t in range(tiles):
                    if t >= 2:
                        act.wait_ge(*added(t - 1))
                    act.activation(ntmp[:, 2 + t % 2, 0:n], src[:, t0 + t, 0:n], ACT.Square).then_inc(squared.s, 1)

            def dve(dve):
                for t in range(tiles):
                    dve.wait_ge(*squared(t + 1))
                    if t == 0:
                        dve.tensor_copy(acc[:, 0:n], ntmp[:, 2, 0:n]).then_inc(added.s, 1)
                    else:
                        dve.wait_ge(*added(t))
                        dve.tensor_tensor(acc[:, 0:n], acc[:, 0:n], ntmp[:, 2 + t % 2, 0:n],
                                          ALU.add).then_inc(added.s, 1)
                dve.wait_ge(*added(tiles))
            stage(None, act, dve)

        def meet():
            stage(lambda e: phase_end(e, "pe"), lambda e: phase_end(e, "act"), lambda e: phase_end(e, "dve"))

        rc = at("rc", o_tmp, [P, TK])
        rs_ = at("rs", o_tmp + 2112, [P, TK])
        rta = at("rta", o_tmp + 4224, [P, 264])
        rtb = at("rtb", o_tmp + 5280, [P, 264])

        def s_mla_project():
            rope_in = sem("rope_in")
            W = 264

            def sp(sp):
                sp.wait_ge(*sem("rope_go")(1))
                for i, t in enumerate((rc, rs_)):
                    sp.dma_start(t[64:96, :], d["rope"][i]).then_inc(rope_in.s, 16)
            q_up, q_raw, rot, kv_up, kv_raw, kv_k, kv_turned, kv_kept = local(
                "st", q_up=4, q_raw=8, rot=8, kv_up=8, kv_raw=8, kv_k=8, kv_turned=8, kv_kept=8)

            def pe(pe):
                for tag, t in [("ncq", 0), ("ncq", 1), ("ncq", 2), ("nck", 0), ("nck", 1)]:
                    xn_ready(pe, tag, t)
                base = BASE["uq"]
                for hd in range(8):
                    s, _, g = slot_of(base, hd // 2)
                    pe.wait_ge(*lo_done(g + 1))
                    if hd >= 2:
                        pe.wait_ge(*q_raw(hd - 1))
                    for kt in range(3):
                        c0 = (hd % 2) * 288 + kt * 96
                        ins = mm3(pe, PS3[0:96, hd % 2, :], s, c0, c0 + 96, cqh[:, kt, 0:T], cql[:, kt, 0:T],
                                  kt == 0, kt == 2)
                    ins.then_inc((chunk_used if hd % 2 else q_up).s, 1)
                    if hd >= 1:
                        rotate(pe, hd - 1)
                rotate(pe, 7)
                base = BASE["ukv"]
                for hd in range(8):
                    s, _, g = slot_of(base, hd // 4)
                    pe.wait_ge(*lo_done(g + 1))
                    if hd >= 1:
                        pe.wait_ge(*kv_raw(hd))
                    for i in range(2):
                        for kt in range(2):
                            c0 = (hd % 4) * 256 + kt * P
                            ins = mm3(pe, PS3[:, i, 0:W], s, c0, c0 + P, ckh[:, kt, i * W:(i + 1) * W],
                                      ckl[:, kt, i * W:(i + 1) * W], kt == 0, kt == 1)
                    ins.then_inc(kv_up.s, 1)
                    if hd % 4 == 3:
                        pe.drain().then_inc(chunk_used.s, 1)
                    pe.wait_ge(*kv_raw(hd + 1))
                    if hd >= 1:
                        pe.wait_ge(*kv_kept(hd))
                    for i in range(4):
                        pe.transpose(PS3[:, 4, i * P:(i + 1) * P], kvf[:, hd % 2, i * P:(i + 1) * P], c_("ident"))
                    pe.transpose(PS3[0:META, 5, 0:P], kvf[:, hd % 2, T:TK], c_("ident")).then_inc(kv_turned.s, 1)
                pe.wait_ge(*sem("ml_kr")(1))
                for i in range(2):
                    ins = pe.matmul(PS3[0:96, 2 + i, 0:W], c_("permm", 0, 96, slice(64, 96)),
                                    km[64:96, 0, i * W:(i + 1) * W], start=True, stop=True, skip_group_check=True)
                ins.then_inc(sem("ml_krot").s, 1)

            def rotate(pe, hd):
                pe.wait_ge(*q_raw(hd + 1))
                if hd >= 1:
                    pe.wait_ge(*rot_read(2 * hd))
                pe.matmul(PS3[0:96, 2, :], c_("permm", 0, 96, slice(64, 96)), qm[64:96, hd, :], start=True,
                          stop=True, skip_group_check=True).then_inc(rot.s, 1)
            rot_read = sem("ml_rotread")

            def act(act):
                base = BASE["uq"]
                for hd in range(8):
                    if hd % 2:
                        act.wait_ge(*chunk_used(base + hd // 2 + 1))
                    else:
                        act.wait_ge(*q_up(hd // 2 + 1))
                    act.activation(qm[:, hd, :], PS3[0:96, hd % 2, :], ACT.Copy).then_inc(q_raw.s, 1)
                    if hd % 2:
                        split_hi(act, base, hd // 2 + 4)
                for hd in range(8):
                    act.wait_ge(*kv_up(hd + 1))
                    if hd >= 2:
                        act.wait_ge(*kv_turned(hd - 1))
                        act.wait_ge(*kv_k(hd - 1))
                    act.activation(halves(kvf[:, hd % 2, :], TK), bank(0, 2, W), ACT.Copy).then_inc(kv_raw.s, 1)
                    if hd % 4 == 3:
                        split_hi(act, BASE["ukv"], hd // 4 + 4)

            def dve(dve):
                ch = Chain(dve, "dve_chain")
                dve.sem_inc(sem("rope_go").s, 1)
                dve.wait_ge(*rope_in(32))

                def turn(dst, i, raw, cols, done=None):
                    ch.link(dve.tensor_tensor(rta[64:96, :], raw, rc[64:96, cols], ALU.mult))
                    ins = dve.tensor_tensor(rtb[64:96, :], i, rs_[64:96, cols], ALU.mult)
                    ch.link(ins)
                    ch.link(dve.tensor_tensor(dst, rta[64:96, :], rtb[64:96, :], ALU.add))
                for hd in range(8):
                    dve.wait_ge(*rot(hd + 1))
                    for i in range(2):
                        c = slice(256 * i, 256 * (i + 1))
                        ch.link(dve.tensor_tensor(rta[64:96, 0:256], qm[64:96, hd, c], rc[64:96, c], ALU.mult))
                        ins = dve.tensor_tensor(rtb[64:96, 0:256], PS3[64:96, 2, c], rs_[64:96, c], ALU.mult)
                        ins.then_inc(rot_read.s, 1)
                        dve.wait_ge(*rot_read(2 * hd + i + 1))
                        ch.link(dve.tensor_tensor(qm[64:96, hd, c], rta[64:96, 0:256], rtb[64:96, 0:256], ALU.add))
                for hd in range(8):
                    dve.wait_ge(*kv_raw(hd + 1))
                    dve.tensor_copy(km[0:64, hd, :], kvf[0:64, hd % 2, :]).then_inc(kv_k.s, 1)
                    dve.wait_ge(*kv_turned(hd + 1))
                    dve.tensor_copy(vm[:, 0:4, hd, :], PS3[:, 4, :].rearrange("p (i n) -> p i n", i=4)[:, :, 64:P])
                    dve.tensor_copy(vm[0:META, 4, hd, :], PS3[0:META, 5, 64:P]).then_inc(kv_kept.s, 1)
                dve.tensor_copy(km[64:96, 0, :], ckv[0:32, 5, :]).then_inc(sem("ml_kr").s, 1)
                dve.wait_ge(*sem("ml_krot")(1))
                for i in range(2):
                    turn(km[64:96, 0, i * W:(i + 1) * W], PS3[64:96, 2 + i, 0:W], km[64:96, 0, i * W:(i + 1) * W],
                         slice(i * W, (i + 1) * W))
                for hd in range(1, 8):
                    dve.tensor_copy(km[64:96, hd, :], km[64:96, 0, :])
            spa, poa = weights("uq")
            spb_, pob = weights("ukv")

            def spx(e):
                spa(e)
                spb_(e)
                sp(e)

            def pox(e):
                poa(e)
                pob(e)
            stage(pe, act, dve, pox, spx)



        def s_latent():
            units = [(hd, i) for hd in range(8) for i in range(4)]
            NU = len(units)
            SC = float(96) ** -0.5
            s_done, masked, mx_done, nb_done, p_done, rs_done, pn_done, t_done, tc_done, pv_done = local(
                "st", s=NU, mask=NU, mx=NU, nb=NU, p=NU, rs=NU, pn=NU, t=NU, tc=NU, pv=NU)
            y_hi, y_lo = local("su", yhi=4, ylo=4)

            def width(u):
                return P * (units[u][1] + 1) + META

            def sbank(u, a, b, rows=slice(0, P)):
                o = 1024 * (u % 2)
                return PS[rows, o + a:o + b]

            def pe(pe):
                phase_end(pe, "pe")

                def scores(u):
                    hd, i = units[u]
                    n = P * (i + 1)
                    if u >= 2:
                        pe.wait_ge(*p_done(u - 1))
                    q = qm[:, hd, i * P:(i + 1) * P]
                    pe.matmul(sbank(u, 0, n), q, km[:, hd, 0:n], start=True, stop=True, skip_group_check=True)
                    pe.matmul(sbank(u, n, n + META), q, km[:, hd, T:TK], start=True, stop=True,
                              skip_group_check=True).then_inc(s_done.s, 1)

                def turn(u):
                    hd, i = units[u]
                    pe.wait_ge(*pn_done(u + 1))
                    if u >= 1:
                        pe.wait_ge(*tc_done(u))
                    for x in range(i + 1):
                        pe.transpose(PS[:, 2048 + x * P:2048 + (x + 1) * P], pm[:, u % 2, x * P:(x + 1) * P],
                                  c_("ident"))
                    n = P * (i + 1)
                    pe.transpose(PS[0:META, 2560:2560 + P], pm[:, u % 2, n:n + META], c_("ident")).then_inc(t_done.s, 1)

                def pv(u):
                    hd, i = units[u]
                    r = 64 * (hd % 2)
                    pe.wait_ge(*tc_done(u + 1))
                    if hd >= 4 and hd % 2 == 0 and i == 0:
                        pe.wait_ge(*y_lo(hd // 2 - 1))
                    o = PS3[r:r + 64, 6 + (hd // 2) % 2, i * P:(i + 1) * P]
                    for x in range(i + 1):
                        pe.matmul(o, vm[:, x, hd, :], pT[:, u % 2, x * P:(x + 1) * P], start=(x == 0),
                                  stop=False, skip_group_check=True)
                    pe.matmul(o, vm[0:META, 4, hd, :], pT[0:META, u % 2, 512:640], start=False, stop=True,
                              skip_group_check=True).then_inc(pv_done.s, 1)
                scores(0)
                scores(1)
                for u in range(NU):
                    if u + 2 < NU:
                        scores(u + 2)
                    turn(u)
                    if u >= 1:
                        pv(u - 1)
                pv(NU - 1)

            def dve(dve):
                phase_end(dve, "dve")

                def top(u):
                    hd, i = units[u]
                    dve.wait_ge(*s_done(u + 1))
                    dve.memset(sbank(u, P * i + 64, P * i + P, slice(0, 64)), NEG).then_inc(masked.s, 1)
                    dve.wait_ge(*masked(u + 1))
                    dve.tensor_reduce(st[:, u % 4:u % 4 + 1], sbank(u, 0, width(u)), AX, ALU.max).then_inc(mx_done.s, 1)
                    dve.wait_ge(*mx_done(u + 1))
                    if u >= 4:
                        dve.wait_ge(*p_done(u - 3))
                    dve.tensor_scalar(st[:, 4 + u % 4:5 + u % 4], st[:, u % 4:u % 4 + 1], -SC, None,
                                      ALU.mult).then_inc(nb_done.s, 1)

                def norm(u):
                    dve.wait_ge(*p_done(u + 1))
                    dve.reciprocal(st[:, 12 + u % 4:13 + u % 4], st[:, 8 + u % 4:9 + u % 4]).then_inc(rs_done.s, 1)
                    dve.wait_ge(*rs_done(u + 1))
                    b = pm[:, u % 2, 0:width(u)]
                    dve.tensor_scalar(b, b, st[:, 12 + u % 4:13 + u % 4], None, ALU.mult).then_inc(pn_done.s, 1)

                def y_out(pair):
                    dve.wait_ge(*y_hi(pair + 1))
                    dve.tensor_tensor(yml_[:, pair, :], PS3[:, 6 + pair % 2, :], ymh[:, pair, :].bitcast(F32),
                                      ALU.subtract).then_inc(y_lo.s, 1)
                top(0)
                for u in range(NU):
                    if u + 1 < NU:
                        top(u + 1)
                    norm(u)
                    if u % 8 == 3 and u >= 8:
                        y_out(u // 8 - 1)
                y_out(3)

            def act(act):
                phase_end(act, "act")
                act.preload_act_table_set("natural_log_exp_and_others")

                def keep(u):
                    n = P * (units[u][1] + 1)
                    act.wait_ge(*t_done(u + 1))
                    if u >= 2:
                        act.wait_ge(*pv_done(u - 1))
                    act.activation(pT[0:META, u % 2, 512:640], PS[0:META, 2560:2560 + P], ACT.Copy)
                    act.activation(pT[:, u % 2, 0:n], PS[:, 2048:2048 + n], ACT.Copy).then_inc(tc_done.s, 1)
                for u in range(NU):
                    act.wait_ge(*nb_done(u + 1))
                    if u >= 2:
                        act.wait_ge(*t_done(u - 1))
                    act.activation(pm[:, u % 2, 0:width(u)], sbank(u, 0, width(u)), ACT.Exp,
                                   bias=st[:, 4 + u % 4:5 + u % 4], scale=SC,
                                   accum_out=st[:, 8 + u % 4:9 + u % 4]).then_inc(p_done.s, 1)
                    if u >= 1:
                        keep(u - 1)
                    if u % 8 == 2 and u >= 8:
                        pair = u // 8 - 1
                        act.wait_ge(*pv_done(8 * pair + 8))
                        act.activation(ymh[:, pair, :], PS3[:, 6 + pair % 2, :], ACT.Copy).then_inc(y_hi.s, 1)
                keep(NU - 1)
                act.wait_ge(*pv_done(NU))
                act.activation(ymh[:, 3, :], PS3[:, 7, :], ACT.Copy).then_inc(y_hi.s, 1)
            stage(pe, act, dve)

        def s_mix():
            base = BASE["wo"]
            a1, a2, mx, mh, ml_ = local("st", a1=DT, a2=DT, mx=DT, hi=DT, lo=DT)

            def pe(pe):
                phase_end(pe, "pe")
                for c in range(8):
                    s, _, g = slot_of(base, c)
                    yh_, yl_ = (ymh, yml_) if c % 2 else (ysbh, ysbl)
                    pe.wait_ge(*lo_done(g + 1))
                    if c >= 4:
                        pe.wait_ge(*mh(c // 2 * 2 - 2))
                        pe.wait_ge(*mx(c // 2 * 2 - 2))
                    for m in range(2):
                        for kt in range(4):
                            c0 = m * 512 + kt * P
                            ins = mm3(pe, PS3[:, 4 * (c // 2 % 2) + 2 * (c % 2) + m, :], s, c0, c0 + P,
                                      yh_[:, kt, :], yl_[:, kt, :], kt == 0, kt == 3)
                    ins.then_inc(chunk_used.s, 1)

            def act(act):
                phase_end(act, "act")
                for c in range(8):
                    split_hi(act, base, c + 4)

            def dve(dve):
                phase_end(dve, "dve")
                for t in range(DT):
                    b = 4 * (t // 2 % 2) + t % 2
                    dve.wait_ge(*chunk_used(base + 2 * (t // 2) + 2))
                    dve.tensor_tensor(mt[:, 0, :], gates[:, t, :], PS3[:, b, :], ALU.mult).then_inc(a1.s, 1)
                    dve.tensor_tensor(mt[:, 1, :], gates[:, 8 + t, :], PS3[:, b + 2, :], ALU.mult).then_inc(a2.s, 1)
                    dve.wait_ge(*a1(t + 1))
                    dve.wait_ge(*a2(t + 1))
                    dve.tensor_tensor(mt[:, 2, :], mt[:, 0, :], mt[:, 1, :], ALU.add).then_inc(mx.s, 1)
                    dve.tensor_tensor(mixh[:, t, :], mt[:, 0, :], mt[:, 1, :], ALU.add).then_inc(mh.s, 1)
                    dve.wait_ge(*mx(t + 1))
                    dve.wait_ge(*mh(t + 1))
                    dve.tensor_tensor(mixl[:, t, :], mt[:, 2, :], mixh[:, t, :].bitcast(F32),
                                      ALU.subtract).then_inc(ml_.s, 1)
                    dve.wait_ge(*ml_(t + 1))
            sp_, pool_ = weights("wo")
            stage(pe, act, dve, pool_, sp_)


        vtm = at("vtm", o_tmp + 12672, [P, 2, T])
        qkf = at("qkf", B + 49296, [P, 8, T])
        mrb = at("mrb", X + 28672, [P, T])
        msq = at("msq", X + 30720, [P, T])
        rst = at("rst", o_tmp + 12288, [P, 24])

        def conv4(dve, name, src, dst, t_in, t_out, cw, cb, ntiles, tap_done, n0):
            for tap in range(4):
                w = v_(cw, tap * ntiles + t_out)
                if tap == 0:
                    ins = dve.tensor_scalar(dst[:, t_out, :], src[:, t_in, 0:T], w, v_(cb, t_out), ALU.mult, ALU.add)
                else:
                    dve.wait_ge(*tap_done(n0 + tap))
                    ins = dve.scalar_tensor_tensor(dst[:, t_out, :], src[:, t_in, tap:T + tap], w, dst[:, t_out, :],
                                                   ALU.mult, ALU.add)
                ins.then_inc(tap_done.s, 1)

        def s_hyif():
            base = BASE["hyif"]
            g_in, col_done, col_kept, if_c, if_bm, if_em = local(
                "post", g_in=2, col=1, colk=1, c=1, bm=1, em=1)

            def pe(pe):
                s, _, g = slot_of(base, 0)
                pe.wait_ge(*lo_done(g + 1))
                for k in range(2):
                    for kt in range(DT):
                        if k == 0:
                            xn_ready(pe, "n4", kt)
                        c0 = kt * 8 + 4 * k
                        ins = mm3(pe, PS3[0:4, 1 + 2 * k, :], s, c0, c0 + 4, xh[:, kt, 0:T], xl[:, kt, 0:T],
                                  kt == 0, kt == DT - 1)
                ins.then_inc(chunk_used.s, 1)

            def pe_columns(pe):
                pe.wait_ge(*if_c(1))
                for j in range(4):
                    ins = pe.transpose(PS3[:, 5, 4 * j:4 * j + 4], rows[:, 4, j * P:(j + 1) * P],
                                       c_("ident", 0, 4, slice(0, 4)))
                ins.then_inc(col_done.s, 1)

            def act(act):
                split_hi(act, base, 4)

            def act_gates(act):
                act.preload_act_table_set("natural_log_exp_and_others")
                ch = Chain(act, "act_chain")
                act.activation(rows[:, 0, :], PS3[0:4, 1, :], ACT.Identity, bias=v_("b_i")[0:4]).then_inc(g_in.s, 1)
                ch.link(act.activation(rows[:, 1, :], PS3[0:4, 3, :], ACT.Identity, bias=v_("b_f")[0:4]))
                ch.link(act.activation(rows[:, 2, :], rows[:, 1, :], ACT.Abs))
                ch.link(act.activation(rows[:, 3, :], rows[:, 2, :], ACT.Exp, scale=-1.0))
                act.activation(rows[:, 2, :], rows[:, 3, :], ACT.Ln, bias=1.0).then_inc(g_in.s, 1)

            def act_em(act):
                act.wait_ge(*if_bm(1))
                act.activation(rows[:, 1, :], rows[:, 2, :], ACT.Exp, scale=-1.0).then_inc(if_em.s, 1)

            def dve_scan(dve):
                ch = Chain(dve, "dve_chain")
                dve.wait_ge(*g_in(2))
                ch.link(dve.scalar_tensor_tensor(rows[:, 1, :], rows[:, 1, :], 0.0, rows[:, 2, :], ALU.min, ALU.subtract))
                ch.link(dve.memset(rows[:, 2, :], 0.0))
                ch.link(dve.tensor_tensor_scan(rows[:, 3, :], rows[:, 1, :], rows[:, 2, :], 0.0, ALU.add, ALU.add))
                dve.tensor_tensor(rows[:, 4, :], rows[:, 0, :], rows[:, 3, :], ALU.subtract).then_inc(if_c.s, 1)
                dve.wait_ge(*if_c(1))
                ch.link(dve.tensor_tensor_scan(rows[:, 5, :], rows[:, 4, :], rows[:, 4, :], NEG, ALU.max, ALU.max))
                dve.tensor_tensor(rows[:, 2, :], rows[:, 3, :], rows[:, 5, :], ALU.add).then_inc(if_bm.s, 1)

            def dve_columns(dve):
                dve.wait_ge(*col_done(1))
                dve.tensor_copy(ccol[:, :, :], PS3[:, 5, 0:16].rearrange("p (j h) -> p j h", j=4)).then_inc(col_kept.s, 1)
            sp_, pool_ = weights("hyif")
            stage(pe, act, None, pool_, sp_)
            return {"pe": (pe_columns,), "act": (act_gates, act_em), "dve": (dve_scan, dve_columns)}

        def s_hyin(gate_steps):
            v_turned, v_kept, taps = local("st", turned=4, kept=4, taps=48)
            pads = sem("pads")
            rw_in = sem("rw_in")

            def evac(act, c, ps):
                if c == 0:
                    act.wait_ge(*pads(3))
                    for i, wt in enumerate((rwa, rwx)):
                        for b in range(2):
                            r = 64 * b
                            act.dma_start(wt[r:r + 64, :, r:r + 64],
                                          d["rw"][i].rearrange("(t b) i j -> b i t j", b=2)[b]).then_inc(rw_in.s, 16)
                if c == 2:
                    gate_steps["act"][0](act)
                if c == 8:
                    gate_steps["act"][1](act)
                if c < 4:
                    o, fn = xrg[:, c, 3:T + 3], ACT.Identity
                elif c < 8:
                    o, fn = grg[:, c - 4, :], ACT.Gelu_apprx_tanh
                elif c < 16:
                    o, fn = qkr[:, c - 8, 3:T + 3], ACT.Identity
                elif c < 20:
                    if c >= 18:
                        act.wait_ge(*v_turned(c - 17))
                    o, fn = vtm[:, c % 2, :], ACT.Identity
                else:
                    o, fn = osg[:, c - 20, :], ACT.Sigmoid
                return act.activation(halves(o, T), ps, fn, bias=v_("hy_b", c))

            def hooks(pe, c):
                if c == 8:
                    gate_steps["pe"][0](pe)
                if 17 <= c < 21:
                    t = c - 17
                    pe.wait_ge(*tile_read["hyin"](16 + t + 1))
                    if t >= 1:
                        pe.wait_ge(*v_kept(t))
                    for i in range(4):
                        ins = pe.transpose(PS3[:, 6, i * P:(i + 1) * P], vtm[:, t % 2, i * P:(i + 1) * P],
                                        c_("ident"))
                    ins.then_inc(v_turned.s, 1)

            def dve(dve):
                dve.memset(xrg[:, :, 0:3], 0.0)
                dve.memset(qkr[:, :, 0:3], 0.0).then_inc(pads.s, 1)
                dve.memset(rwa[:, :, :], 0.0).then_inc(pads.s, 1)
                dve.memset(rwx[:, :, :], 0.0).then_inc(pads.s, 1)
                for t in range(4):
                    dve.wait_ge(*tile_read["hyin"](t + 1))
                    conv4(dve, "rg", xrg, xc, t, t, "rg_cw", "rg_cb", 4, taps, 4 * t)
                    if t == 2:
                        gate_steps["dve"][0](dve)
                for t in range(8):
                    dve.wait_ge(*tile_read["hyin"](8 + t + 1))
                    conv4(dve, "ml", qkr, qkf, t, t, "ml_cw", "ml_cb", 8, taps, 16 + 4 * t)
                    if t == 1:
                        gate_steps["dve"][1](dve)
                for t in range(4):
                    dve.wait_ge(*v_turned(t + 1))
                    dve.tensor_copy(vml[:, 0:4, t * P:(t + 1) * P],
                                    PS3[:, 6, :].rearrange("p (i n) -> p i n", i=4)).then_inc(v_kept.s, 1)

            project("hyin", "n4", lambda c: T, evac, hooks=hooks, dve_=dve)

        def s_rglru():
            g_done, silu, ksc, rx, lam, a_done, th_done, v_done, s_done, rg_loga = local(
                "st", gates=4, silu=1, kscale=1, rx=4, lam=1, a=1, th=1, v=1, s=1, loga=1)

            def flat(x):
                return x[:, :, :].rearrange("p a b -> p (a b)")

            def pe(pe):
                phase_end(pe, "pe")
                pe.wait_ge(*sem("rw_in")(64))
                for t in range(4):
                    pe.matmul(PS3[:, t, :], rwa[:, t, :], xc[:, t, :], start=True, stop=True)
                    pe.matmul(PS3[:, 4 + t, :], rwx[:, t, :], xc[:, t, :], start=True, stop=True).then_inc(g_done.s, 1)

            def act(act):
                phase_end(act, "act")
                ch = Chain(act, "act_chain")
                act.preload_act_table_set("natural_log_exp_and_others")
                lamv = vec[:, VOFF["rg_lam"]:VOFF["rg_lam"] + 4]
                ch.link(act.activation(rst[:, 0:4], lamv, ACT.Abs))
                ch.link(act.activation(rst[:, 4:8], rst[:, 0:4], ACT.Exp, scale=-1.0))
                act.activation(rst[:, 8:12], rst[:, 4:8], ACT.Ln, bias=1.0).then_inc(lam.s, 1)
                act.preload_act_table_set("sigmoid_and_others")
                for t in range(4):
                    act.wait_ge(*g_done(t + 1))
                    act.activation(rga[:, t, :], PS3[:, t, :], ACT.Sigmoid, bias=v_("rg_ba", t))
                    act.activation(rgi[:, t, :], PS3[:, 4 + t, :], ACT.Sigmoid, bias=v_("rg_bx", t)).then_inc(rx.s, 1)
                act.preload_act_table_set("exp_and_others")
                act.wait_ge(*rg_loga(1))
                act.activation(flat(rga), flat(rgt), ACT.Exp).then_inc(a_done.s, 1)
                act.activation(flat(rgu), flat(rgt), ACT.Tanh, scale=-1.0).then_inc(th_done.s, 1)
                act.wait_ge(*v_done(1))
                act.activation(flat(rgu), flat(rgt), ACT.Sqrt).then_inc(s_done.s, 1)
                phase_end(act, "act")
                act.preload_act_table_set("silu_and_others")
                act.activation(qkc[:, :, :].rearrange("p a b -> p (a b)"), flat(qkf), ACT.Silu).then_inc(silu.s, 1)

            def dve(dve):
                phase_end(dve, "dve")
                ch = Chain(dve, "dve_chain")
                lamv = vec[:, VOFF["rg_lam"]:VOFF["rg_lam"] + 4]
                ch.link(dve.tensor_scalar(rst[:, 12:16], lamv, -1.0, 0.0, ALU.mult, ALU.max))
                dve.wait_ge(*lam(1))
                ch.link(dve.tensor_tensor(rst[:, 16:20], rst[:, 12:16], rst[:, 8:12], ALU.add))
                ch.link(dve.tensor_scalar(rst[:, 20:24], rst[:, 16:20], -8.0, None, ALU.mult))
                for t in range(4):
                    dve.wait_ge(*rx(t + 1))
                    ins = dve.tensor_scalar(rgt[:, t, :], rga[:, t, :], rst[:, 20 + t:21 + t], None, ALU.mult)
                ins.then_inc(rg_loga.s, 1)
                ch.link(dve.tensor_tensor(flat(rgi), flat(rgi), flat(xc), ALU.mult))
                dve.wait_ge(*a_done(1))
                dve.wait_ge(*th_done(1))
                ch.link(dve.tensor_tensor(flat(rgt), flat(rga), flat(rga), ALU.mult))
                ch.link(dve.scalar_tensor_tensor(flat(rgt), flat(rgt), 1.0, flat(rgu), ALU.add, ALU.mult))
                dve.tensor_scalar(flat(rgt), flat(rgt), 1e-34, None, ALU.max).then_inc(v_done.s, 1)
                dve.wait_ge(*s_done(1))
                ch.link(dve.tensor_tensor(flat(rgi), flat(rgi), flat(rgu), ALU.mult))
                for t in range(4):
                    ins = dve.tensor_tensor_scan(rgt[:, t, :], rga[:, t, :], rgi[:, t, :], 0.0, ALU.mult, ALU.add)
                ch.link(ins)
                phase_end(dve, "dve")
                dve.wait_ge(*silu(1))
                ch.link(dve.tensor_tensor(flat(grg), flat(grg), flat(rgt), ALU.mult))
                ch.link(dve.tensor_copy(yh[:, 0:4, :], grg[:, :, :]))
                ch.link(dve.tensor_tensor(yl[:, 0:4, :], grg[:, :, :], yh[:, 0:4, :].bitcast(F32), ALU.subtract))
                dve.tensor_scalar(qkc[:, 4:8, :], qkc[:, 4:8, :], float(P) ** -0.5, None, ALU.mult).then_inc(ksc.s, 1)

            def pe2(pe_):
                pe(pe_)
                phase_end(pe_, "pe")
            stage(pe2, act, dve)

        def s_mlstm():
            units = [(hd, j) for hd in range(4) for j in range(4)]
            (s_done, m_done, w_done, st_done, cut, pv_done, nm_done, abs_done, mx_done, rec_done, num_done, sq_done,
             ss_done, ln_done, rb_done, t_done, p_done, h_done, l_done) = local(
                "st", s=16, m=4, w=16, st=16, cut=16, pv=16, nm=4, abs=4, mx=4, rec=4, num=4, sq=4, ss=4, ln=4,
                rb=4, t=4, p=4, h=4, l=4)

            def pe(pe):
                phase_end(pe, "pe")

                def spread(hd):
                    if hd >= 2:
                        pe.wait_ge(*mx_done(hd - 1))
                    pe.matmul(PS3[:, 2 + hd % 2, :], c_("sel", hd * P, (hd + 1) * P, slice(0, 4)), rows[:, 5, :],
                              start=True, stop=True, skip_group_check=True).then_inc(m_done.s, 1)

                def scores(u):
                    hd, j = units[u]
                    if u >= 2:
                        pe.wait_ge(*st_done(u - 1))
                    pe.matmul(PS3[:, u % 2, j * P:T], qkc[:, 4 + hd, j * P:(j + 1) * P], qkc[:, hd, j * P:T],
                              start=True, stop=True, skip_group_check=True).then_inc(s_done.s, 1)

                def sums(u):
                    hd, j = units[u]
                    pe.wait_ge(*cut(u + 1))
                    if hd >= 2 and j == 0:
                        pe.wait_ge(*num_done(hd - 1))
                        pe.wait_ge(*abs_done(hd - 1))
                    pe.matmul(PS3[:, 4 + hd % 2, j * P:T], vml[:, j, hd * P:(hd + 1) * P], mst[:, u % 4, j * P:T],
                              start=j == 0, stop=j == 3, skip_group_check=True)
                    pe.matmul(PS3[:, 6 + hd % 2, j * P:T], c_("ones"), mst[:, u % 4, j * P:T],
                              start=j == 0, stop=j == 3, skip_group_check=True).then_inc(pv_done.s, 1)

                def finish(hd):
                    pe.wait_ge(*w_done(4 * hd + 4))
                    pe.matmul(PS3[:, 2 + hd % 2, :], c_("sel", hd * P, (hd + 1) * P, slice(0, 4)), rows[:, 1, :],
                              start=True, stop=True, skip_group_check=True).then_inc(nm_done.s, 1)

                def squares(hd):
                    pe.wait_ge(*sq_done(hd + 1))
                    pe.matmul(PS3[:, 6 + hd % 2, :], c_("ones"), msq[:, :], start=True, stop=True,
                              skip_group_check=True).then_inc(ss_done.s, 1)
                spread(0)
                scores(0)
                for u in range(16):
                    hd, j = units[u]
                    if j == 3 and hd < 3:
                        spread(hd + 1)
                    if u + 1 < 16:
                        scores(u + 1)
                    sums(u)
                    if j == 3:
                        finish(hd)
                    if j == 2 and hd >= 1:
                        squares(hd - 1)
                squares(3)

            def act(act):
                phase_end(act, "act")
                act.preload_act_table_set("natural_log_exp_and_others")

                def w(u):
                    hd, j = units[u]
                    act.wait_ge(*m_done(hd + 1))
                    if u >= 2:
                        act.wait_ge(*st_done(u - 1))
                    act.activation(msw[:, u % 2, j * P:T], PS3[:, 2 + hd % 2, j * P:T], ACT.Exp,
                                   bias=ccol[:, j, hd:hd + 1], scale=-1.0).then_inc(w_done.s, 1)

                def magnitude(hd):
                    act.wait_ge(*pv_done(4 * hd + 4))
                    if hd >= 1:
                        act.wait_ge(*l_done(hd))
                    act.activation(mden[:, :], PS3[:, 6 + hd % 2, :], ACT.Abs).then_inc(abs_done.s, 1)

                def square(hd):
                    act.wait_ge(*num_done(hd + 1))
                    act.activation(msq[:, :], mnum[:, hd % 2, :], ACT.Square).then_inc(sq_done.s, 1)

                def rms(hd):
                    act.wait_ge(*ss_done(hd + 1))
                    act.activation(mrb[:, :], PS3[:, 6 + hd % 2, :], ACT.Ln, bias=epsc[:, 0:1],
                                   scale=1.0 / P).then_inc(ln_done.s, 1)
                    act.wait_ge(*ln_done(hd + 1))
                    act.activation(mrb[:, :], mrb[:, :], ACT.Exp, scale=-0.5).then_inc(rb_done.s, 1)
                steps = {0: magnitude, 2: square, 3: rms}
                for u in range(16):
                    hd, j = units[u]
                    w(u)
                    if hd >= 1 and j in steps:
                        steps[j](hd - 1)
                for step in steps.values():
                    step(3)

            def dve(dve):
                phase_end(dve, "dve")

                def divide(hd):
                    dve.wait_ge(*nm_done(hd + 1))
                    dve.wait_ge(*abs_done(hd + 1))
                    dve.tensor_tensor(mden[:, :], mden[:, :], PS3[:, 2 + hd % 2, :], ALU.max).then_inc(mx_done.s, 1)
                    dve.wait_ge(*mx_done(hd + 1))
                    dve.reciprocal(mden[:, :], mden[:, :]).then_inc(rec_done.s, 1)
                    dve.wait_ge(*rec_done(hd + 1))
                    dve.tensor_tensor(mnum[:, hd % 2, :], mden[:, :], PS3[:, 4 + hd % 2, :],
                                      ALU.mult).then_inc(num_done.s, 1)

                def gate(hd):
                    dve.wait_ge(*rb_done(hd + 1))
                    dve.scalar_tensor_tensor(mden[:, :], mnum[:, hd % 2, :], v_("ml_norm", hd), mrb[:, :],
                                             ALU.mult, ALU.mult).then_inc(t_done.s, 1)
                    dve.wait_ge(*t_done(hd + 1))
                    dve.tensor_tensor(mnum[:, hd % 2, :], mden[:, :], osg[:, hd, :], ALU.mult).then_inc(p_done.s, 1)
                    dve.tensor_tensor(yh[:, 4 + hd, :], mden[:, :], osg[:, hd, :], ALU.mult).then_inc(h_done.s, 1)
                    dve.wait_ge(*p_done(hd + 1))
                    dve.wait_ge(*h_done(hd + 1))
                    dve.tensor_tensor(yl[:, 4 + hd, :], mnum[:, hd % 2, :], yh[:, 4 + hd, :].bitcast(F32),
                                      ALU.subtract).then_inc(l_done.s, 1)
                for u in range(16):
                    hd, j = units[u]
                    dve.wait_ge(*s_done(u + 1))
                    dve.wait_ge(*w_done(u + 1))
                    if u >= 4:
                        dve.wait_ge(*pv_done(u - 3))
                    dve.tensor_tensor(mst[:, u % 4, j * P:T], msw[:, u % 2, j * P:T], PS3[:, u % 2, j * P:T],
                                      ALU.mult).then_inc(st_done.s, 1)
                    if hd >= 1 and j == 1:
                        divide(hd - 1)
                    if hd >= 2 and j == 0:
                        gate(hd - 2)
                gate(2)
                divide(3)
                gate(3)

            def pool(pool):
                for u in range(16):
                    hd, j = units[u]
                    pool.wait_ge(*st_done(u + 1))
                    b = mst[:, u % 4, P * j:P * (j + 1)]
                    pool.affine_select(out=b, in_=b, pattern=[[1, P]], compare_op=ALU.is_ge, fill=0.0, base=0,
                                       channel_multiplier=-1).then_inc(cut.s, 1)
            stage(pe, act, dve, pool)

        def s_ple_proj(layer, tag, gain):
            name = f"pp{layer}"
            p_in, ph_, pl_, read, p_done = local("pp", p_in=32, hi=1, lo=1, read=DT, done=DT)

            def act_early(act):
                for kt in range(2):
                    act.dma_start(ptx[:, kt, :], d["pT"][layer, kt]).then_inc(p_in.s, 16)
                act.wait_ge(*p_in(32))
                act.activation(ph[:, :, :], ptx[:, :, :], ACT.Copy).then_inc(ph_.s, 1)

            def dve_early(dve):
                dve.wait_ge(*ph_(1))
                dve.tensor_tensor(pl[:, :, :], ptx[:, :, :], ph[:, :, :].bitcast(F32), ALU.subtract).then_inc(pl_.s, 1)
            s_prenorm(tag, gain, T, early=(act_early, dve_early))
            base = BASE[name]

            def pe(pe):
                pe.wait_ge(*pl_(1))
                for t in range(DT):
                    s, _, g = slot_of(base, t // 4)
                    pe.wait_ge(*lo_done(g + 1))
                    if t == 6:
                        xn_ready(pe, tag, 0)
                    for kt in range(2):
                        c0 = (t % 4) * 256 + kt * P
                        ins = mm3(pe, PS3[:, t, :], s, c0, c0 + P, ph[:, kt, :], pl[:, kt, :], kt == 0, kt == 1)
                    ins.then_inc(p_done.s, 1)
                    if t % 4 == 3:
                        pe.drain().then_inc(chunk_used.s, 1)
                pe.wait_ge(*read(5))

            def act(act):
                for t in range(DT):
                    act.wait_ge(*p_done(t + 1))
                    act.activation(prj[:, t, :], PS3[:, t, :], ACT.Copy).then_inc(read.s, 1)
                    if t % 4 == 3:
                        split_hi(act, base, t // 4 + 4)
            sp, pool = weights(name)
            stage(pe, act, None, pool, sp)

        def s_ple_gate(layer, xn, last):
            name = f"pg{layer}"
            own, added, freed = local("pg", own=2 * DT - 1, added=DT, freed=DT)

            def evac(act, c, ps):
                if c == 0:
                    act.preload_act_table_set("sigmoid_and_others")
                if c >= 2:
                    act.wait_ge(*freed(c - 1))
                return act.activation(halves(sgp[:, c % 2, :], T), ps, ACT.Sigmoid)

            def dve(dve):
                for t in range(DT):
                    dve.wait_ge(*tile_read[name](t + 1))
                    dve.tensor_tensor(prj[:, t, :], prj[:, t, :], sgp[:, t % 2, :], ALU.mult).then_inc(freed.s, 1)
                    dve.wait_ge(*freed(t + 1))
                    dve.tensor_tensor(h[:, t, 0:T], h[:, t, 0:T], prj[:, t, :], ALU.add).then_inc(added.s, 1)
                    if last:
                        continue
                    dve.wait_ge(*added(t + 1))
                    if t == 0:
                        dve.tensor_tensor(acc[:, 0:T], h[:, t, 0:T], h[:, t, 0:T], ALU.mult).then_inc(own.s, 1)
                        dve.wait_ge(*own(1))
                        continue
                    dve.tensor_tensor(sq[:, 0:T], h[:, t, 0:T], h[:, t, 0:T], ALU.mult).then_inc(own.s, 1)
                    dve.wait_ge(*own(2 * t))
                    dve.tensor_tensor(acc[:, 0:T], acc[:, 0:T], sq[:, 0:T], ALU.add).then_inc(own.s, 1)
                    dve.wait_ge(*own(2 * t + 1))
            project(name, xn, lambda c: T, evac, dve_=dve)
            if last:
                def sp(sp):
                    for t in range(DT):
                        sp.wait_ge(*added(t + 1))
                        sp.dma_start(out[t], h[:, t, 0:T]).then_inc(sem("out_landed").s, 16)
                    sp.wait_ge(*sem("out_landed")(16 * DT))
                SP.append(sp)

        pos1 = at("pos1", B + 86016, [1, T], mybir.dt.int32)
        posf = at("posf", B + 88064 + 6144, [1, T])

        MAGIC = 1.5 * 2.0 ** 23
        C1, C2 = 6.28125, 1.9350051879882812e-3
        C3 = 2 * math.pi - C1 - C2
        PI = 3.1415925

        def angles(dve, p_in, pf, pb, an_r, an_o):
            ch = Chain(dve, "dve_chain")
            dve.wait_ge(*p_in(16))
            dve.tensor_copy(posf[:, :], pos1[:, :]).then_inc(pf.s, 1)
            dve.wait_ge(*pb(1))
            ch.link(dve.tensor_scalar(ang[:, 0, :], PS3[:, 7, :], c_("invf"), None, ALU.mult))
            a, k, r = ang[:, 0, :], ang[:, 1, :], ang[:, 2, :]
            for i in range(2):
                if i:
                    dve.wait_ge(*an_o(1))
                ch.link(dve.tensor_scalar(k, a, 1 / (2 * math.pi), 0.25 * i, ALU.mult, ALU.add))
                ch.link(dve.tensor_scalar(k, k, MAGIC, None, ALU.add))
                ch.link(dve.tensor_scalar(k, k, -MAGIC, None, ALU.add))
                ch.link(dve.scalar_tensor_tensor(r, k, -C1, a, ALU.mult, ALU.add))
                ch.link(dve.scalar_tensor_tensor(r, k, -C2, r, ALU.mult, ALU.add))
                ch.link(dve.scalar_tensor_tensor(r, k, -C3, r, ALU.mult, ALU.add))
                if i:
                    ch.link(dve.tensor_scalar(r, r, math.pi / 2, None, ALU.add))
                dve.tensor_scalar(r, r, PI, -PI, ALU.min, ALU.max).then_inc(an_r.s, 1)
            dve.wait_ge(*an_o(2))

        def s_qkv():
            (v_turned, v_kept, sqd, ssd, lnd, rbd, nd, rotd, m1, m2, fin, dupd, dupk) = local(
                "st", turned=2, kept=2, sq=10, ss=10, ln=10, rb=10, n=10, rot=10, m1=10, m2=10, fin=10, dup=4, dupk=4)
            p_in, pf, pb, an_r, an_o = local("an", p_in=16, pf=1, pb=1, r=2, o=2)

            def dma_early(act):
                act.dma_start(pos1[:, :], d["pos"]).then_inc(p_in.s, 16)
            s_prenorm("n6", "norm_mix1", T, early=(dma_early, None))

            def tile(t):
                return qa[:, t, :] if t < 8 else ka[:, t - 8, :]

            def evac(act, c, ps):
                return act.activation(halves(tile(c) if c < 10 else vtm[:, c % 2, :], T), ps, ACT.Copy)

            def ss(pe, t):
                pe.wait_ge(*sqd(t + 1))
                if t >= 2:
                    pe.wait_ge(*lnd(t - 1))
                pe.matmul(PS3[:, 1 + 2 * (t % 2), :], c_("blk64"), qsq[:, t % 2, :], start=True,
                          stop=True).then_inc(ssd.s, 1)

            def half_turn(pe, t):
                pe.wait_ge(*nd(t + 1))
                if t >= 2:
                    pe.wait_ge(*m2(t - 1))
                pe.matmul(PS3[:, 5 + 2 * (t % 2), :], c_("permh"), tile(t), start=True, stop=True).then_inc(rotd.s, 1)

            def hooks(pe, c):
                if c == 0:
                    pe.wait_ge(*pf(1))
                    pe.matmul(PS3[:, 7, :], c_("ones", 0, P, slice(0, 1)), posf[:, :], start=True, stop=True,
                              skip_group_check=True).then_inc(pb.s, 1)
                if 1 <= c < 11:
                    ss(pe, c - 1)
                if 3 <= c < 13:
                    half_turn(pe, c - 3)
                if c in (11, 12):
                    t = c - 11
                    pe.wait_ge(*tile_read["qkv"](10 + t + 1))
                    if t:
                        pe.wait_ge(*v_kept(1))
                    for i in range(4):
                        ins = pe.transpose(PS3[:, 6, i * P:(i + 1) * P], vtm[:, t, i * P:(i + 1) * P], c_("ident"))
                    ins.then_inc(v_turned.s, 1)
                if c == 12:
                    pe.wait_ge(*fin(10))
                    for kv in range(4):
                        pe.matmul(PS3[:, kv, :], c_(f"dup{kv % 2}"), ka[:, kv // 2, :], start=True,
                                  stop=True).then_inc(dupd.s, 1)

            def after(act, c):
                if c < 10:
                    act.wait_ge(*tile_read["qkv"](c + 1))
                    if c >= 2:
                        act.wait_ge(*ssd(c - 1))
                    act.activation(qsq[:, c % 2, :], tile(c), ACT.Square).then_inc(sqd.s, 1)
                if c in (1, 2):
                    if c == 1:
                        act.preload_act_table_set("silu_and_others")
                    act.wait_ge(*an_r(c))
                    act.activation((sinr, cosr)[c - 1][:, :], ang[:, 2, :], ACT.Sin).then_inc(an_o.s, 1)
                if c == 2:
                    act.preload_act_table_set("natural_log_exp_and_others")
                if c >= 2:
                    t = c - 2
                    act.wait_ge(*ssd(t + 1))
                    if t >= 2:
                        act.wait_ge(*nd(t - 1))
                    act.activation(qrb[:, t % 2, :], PS3[:, 1 + 2 * (t % 2), :], ACT.Ln, bias=epsc[:, 0:1],
                                   scale=1.0 / 64).then_inc(lnd.s, 1)
                    act.wait_ge(*lnd(t + 1))
                    act.activation(qrb[:, t % 2, :], qrb[:, t % 2, :], ACT.Exp, scale=-0.5).then_inc(rbd.s, 1)
                if c == 11:
                    for kv in range(4):
                        act.wait_ge(*dupd(kv + 1))
                        act.activation(kdup[:, kv, :], PS3[:, kv, :], ACT.Copy).then_inc(dupk.s, 1)

            def dve(dve):
                angles(dve, p_in, pf, pb, an_r, an_o)

                def norm(t):
                    dve.wait_ge(*rbd(t + 1))
                    g = v_("at_qn") if t < 8 else v_("at_kn")
                    dve.scalar_tensor_tensor(tile(t), tile(t), g, qrb[:, t % 2, :], ALU.mult, ALU.mult).then_inc(nd.s, 1)

                def rot(t):
                    dve.wait_ge(*nd(t + 1))
                    dve.tensor_tensor(qt1[:, t % 2, :], tile(t), cosr[:, :], ALU.mult).then_inc(m1.s, 1)
                    dve.wait_ge(*rotd(t + 1))
                    dve.tensor_tensor(qt2[:, t % 2, :], sinr[:, :], PS3[:, 5 + 2 * (t % 2), :], ALU.mult).then_inc(m2.s, 1)
                    dve.wait_ge(*m1(t + 1))
                    dve.wait_ge(*m2(t + 1))
                    dve.tensor_tensor(tile(t), qt1[:, t % 2, :], qt2[:, t % 2, :], ALU.add).then_inc(fin.s, 1)
                    dve.wait_ge(*fin(t + 1))

                def keep(t):
                    dve.wait_ge(*v_turned(t + 1))
                    dve.tensor_copy(va[:, 0:4, t * P:(t + 1) * P],
                                    PS3[:, 6, :].rearrange("p (i n) -> p i n", i=4)).then_inc(v_kept.s, 1)
                norm(0)
                for t in range(8):
                    norm(t + 1)
                    rot(t)
                keep(0)
                norm(9)
                rot(8)
                rot(9)
                keep(1)
            project("qkv", "n6", lambda c: T, evac, hooks=hooks, dve_=dve, after=after)

        def s_window():
            units = [(n, g) for n in range(4) for g in range(4)]
            NU = 16
            s_done, sc, mx, mm, sub, p_done, es, den, rec, pn, td, tcd, pvd, yhi, ylo = local(
                "st", s=NU, sc=NU, mx=NU, mm=NU, sub=2 * NU, p=NU, es=NU, den=NU, rec=NU, pn=NU, t=NU,
                tc=NU, pv=NU, yhi=NU, ylo=NU)

            def k0(u):
                return P if units[u][0] == 0 else 0

            def place(x):
                return 2 * (x % 2) + x // 2

            def sc_ps(u, lo_=0):
                return PS[:, 1024 * (u % 2):1024 * (u % 2) + 1024].rearrange("p (g k) -> p g k", g=4)[:, :, lo_:]

            def pe(pe):
                phase_end(pe, "pe")

                def scores(u):
                    n, g = units[u]
                    if u >= 2:
                        pe.wait_ge(*sc(u - 1))
                    for x in range(4):
                        hq = 4 * g + x
                        r = 64 * (hq % 2)
                        o = 1024 * (u % 2) + 256 * place(x)
                        ins = pe.matmul(PS[:, o + k0(u):o + 256], qa[r:r + 64, hq // 2, n * P:(n + 1) * P],
                                        kdup[r:r + 64, g, (n - 1) * P + k0(u):(n + 1) * P],
                                        start=True, stop=True, skip_group_check=True)
                    ins.then_inc(s_done.s, 1)

                def turn(u):
                    pe.wait_ge(*pn(u + 1))
                    if u >= 1:
                        pe.wait_ge(*tcd(u))
                    for x in range(4):
                        for b in range(k0(u) // P, 2):
                            ins = pe.transpose(PS[:, 2048 + (2 * x + b) * P:2048 + (2 * x + b + 1) * P],
                                            asx[:, u % 2, x, b * P:(b + 1) * P], c_("ident"))
                    ins.then_inc(td.s, 1)

                def pv(u):
                    n, g = units[u]
                    pe.wait_ge(*tcd(u + 1))
                    if u >= 2:
                        pe.wait_ge(*ylo(u - 1))
                    for x in range(4):
                        hq = 4 * g + x
                        r = 64 * (hq % 2)
                        o = PS3[r:r + 64, 6 + u % 2, (x // 2) * P:(x // 2 + 1) * P]
                        for b in range(k0(u) // P, 2):
                            ins = pe.matmul(o, va[:, n - 1 + b, g * 64:(g + 1) * 64],
                                            apt[:, u % 2, (2 * place(x) + b) * P:(2 * place(x) + b + 1) * P],
                                            start=b == k0(u) // P, stop=b == 1, skip_group_check=True)
                    ins.then_inc(pvd.s, 1)
                scores(0)
                scores(1)
                for u in range(NU):
                    if u + 2 < NU:
                        scores(u + 2)
                    turn(u)
                    if u >= 1:
                        pv(u - 1)
                pv(NU - 1)

            def col(u, k):
                return ast_[:, u % 2, k, :]

            def dve(dve):
                phase_end(dve, "dve")

                def top(u):
                    n, g = units[u]
                    a = asx[:, u % 2, :, k0(u):256]
                    w = 256 - k0(u)
                    dve.wait_ge(*s_done(u + 1))
                    if u >= 2:
                        dve.wait_ge(*td(u - 1))
                    band = c_("band", k0(u), 256)
                    band4 = bass.AP(tensor=band.tensor, offset=band.offset,
                                    ap=[band.ap[0], [0, 4], [1, w]])
                    dve.scalar_tensor_tensor(a, sc_ps(u, k0(u)), 0.125, band4, ALU.mult, ALU.add).then_inc(sc.s, 1)
                    dve.wait_ge(*sc(u + 1))
                    dve.tensor_reduce(col(u, 0), a, AX, ALU.max).then_inc(mx.s, 1)
                    dve.wait_ge(*mx(u + 1))
                    sk = vec[:, VOFF["sinks"] + 4 * g:VOFF["sinks"] + 4 * g + 4]
                    dve.tensor_tensor(col(u, 1), col(u, 0), sk, ALU.max).then_inc(mm.s, 1)
                    dve.wait_ge(*mm(u + 1))
                    dve.tensor_tensor(col(u, 2), sk, col(u, 1), ALU.subtract).then_inc(sub.s, 1)
                    dve.tensor_scalar(col(u, 6), col(u, 1), -1.0, None, ALU.mult).then_inc(sub.s, 1)

                def norm(u):
                    a = asx[:, u % 2, :, k0(u):256]
                    w = 256 - k0(u)
                    dve.wait_ge(*p_done(u + 1))
                    dve.wait_ge(*es(u + 1))
                    dve.tensor_tensor(col(u, 5), col(u, 4), col(u, 3), ALU.add).then_inc(den.s, 1)
                    dve.wait_ge(*den(u + 1))
                    dve.reciprocal(col(u, 7), col(u, 5)).then_inc(rec.s, 1)
                    dve.wait_ge(*rec(u + 1))
                    m = col(u, 7)
                    m4 = bass.AP(tensor=m.tensor, offset=m.offset, ap=[m.ap[0], [1, 4], [0, w]])
                    dve.tensor_tensor(a, a, m4, ALU.mult).then_inc(pn.s, 1)

                def y_out(u):
                    n, g = units[u]
                    dve.wait_ge(*yhi(u + 1))
                    dve.tensor_tensor(ayl[:, 2 * g:2 * g + 2, n * P:(n + 1) * P],
                                      PS3[:, 6 + u % 2, 0:256].rearrange("p (a q) -> p a q", a=2),
                                      ayh[:, 2 * g:2 * g + 2, n * P:(n + 1) * P].bitcast(F32),
                                      ALU.subtract).then_inc(ylo.s, 1)
                top(0)
                for u in range(NU):
                    if u + 1 < NU:
                        top(u + 1)
                    norm(u)
                    if u >= 2:
                        y_out(u - 2)
                y_out(NU - 2)
                y_out(NU - 1)

            def act(act):
                phase_end(act, "act")
                act.preload_act_table_set("natural_log_exp_and_others")

                def probs(u):
                    act.wait_ge(*sub(2 * u + 2))
                    act.activation(col(u, 3), col(u, 2), ACT.Exp).then_inc(es.s, 1)
                    for x in range(4):
                        a = asx[:, u % 2, x, k0(u):256]
                        ins = act.activation(a, a, ACT.Exp, bias=ast_[:, u % 2, 6, x:x + 1],
                                             accum_out=ast_[:, u % 2, 4, x:x + 1])
                    ins.then_inc(p_done.s, 1)

                def keep(u):
                    act.wait_ge(*td(u + 1))
                    if u >= 2:
                        act.wait_ge(*pvd(u - 1))
                    sl = PS[:, 2048:3072].rearrange("p (x k) -> p x k", x=4)[:, :, k0(u):256]
                    act.activation(apt[:, u % 2, :].rearrange("p (x k) -> p x k", x=4)[:, :, k0(u):256], sl,
                                   ACT.Copy).then_inc(tcd.s, 1)

                def y_out(u):
                    n, g = units[u]
                    act.wait_ge(*pvd(u + 1))
                    act.activation(ayh[:, 2 * g:2 * g + 2, n * P:(n + 1) * P],
                                   PS3[:, 6 + u % 2, 0:256].rearrange("p (a q) -> p a q", a=2),
                                   ACT.Copy).then_inc(yhi.s, 1)
                probs(0)
                for u in range(NU):
                    if u + 1 < NU:
                        probs(u + 1)
                    keep(u)
                    if u >= 1:
                        y_out(u - 1)
                y_out(NU - 1)
            stage(pe, act, dve)


        def s_dump(ap, n):
            def sp(sp):
                sp.wait_ge(*sem("dumpgo")(3))
                sp.dma_start(out[0:ap.shape[0], 0:n], ap).then_inc(sem("dumped").s, 16)
                sp.wait_ge(*sem("dumped")(16))

            def mk(who):
                def g(e):
                    phase_end(e, who)
                    e.sem_inc(sem("dumpgo").s, 1)
                return g
            stage(mk("pe"), mk("act"), mk("dve"), None, sp)

        def set_eps():
            def dve(dve):
                dve.memset(epsc[:, 0:1], EPS)
                dve.memset(epsc[:, 1:2], 1.0)
            def e(who):
                return lambda eng: phase_end(eng, who)
            DV.append(dve)
            PE.append(e("pe")); AC.append(e("act")); DV.append(e("dve"))

        set_eps()
        s_load()
        plan(locals())

        block = ctx.enter_context(nc.Block())

        @block.sync
        def _(sp):
            for s in SP:
                s(sp)

        @block.gpsimd
        def _(pool):
            for s in PO:
                s(pool)

        @block.scalar
        def _(act):
            for s in AC:
                s(act)

        @block.vector
        def _(dve):
            for s in DV:
                s(dve)

        @block.tensor
        def _(pe):
            for s in PE:
                s(pe)


def plan(L):
    s_prenorm, s_gate_up, s_out, rhs_hid, s_postnorm, s_dump = (L[k] for k in
        "s_prenorm s_gate_up s_out rhs_hid s_postnorm s_dump".split())
    s_prenorm("n1", "ffn1_pre", TK)
    if UPTO == 0:
        return s_dump(L["xh"][:, :, :].rearrange("p a b -> p (a b)").bitcast(F32), DT * TK)
    s_gate_up("f1gu", "n1", TK)
    s_out("f1dn", (6, 6, 5, 5), rhs_hid(TK), TK, 2, False)
    s_postnorm("p1", "ffn1_post", TK, 0.5)
    if UPTO == 1:
        return s_dump(L["h"][:, :, :].rearrange("p a b -> p (a b)"), DT * TK)
    def fl(name, n, f=F32):
        a = L[name][:, :, :].rearrange("p a b -> p (a b)")
        return s_dump(a.bitcast(F32) if f != F32 else a, n)
    s_prenorm("n2", "mix_pre", TK)
    L["s_win"]()
    L["s_stick"]()
    if UPTO == 2:
        return fl("ysbh", 4 * T, F32R)
    L["meet"]()
    L["s_small_squares"]("sq_cq", L["ckv"], 0, 3, TK)
    s_prenorm("ncq", "q_norm", TK, k=384, tiles=3, src=L["ckv"], dst=(L["cqh"], L["cql"]))
    L["meet"]()
    L["s_small_squares"]("sq_ck", L["ckv"], 3, 2, TK)
    s_prenorm("nck", "kv_norm", TK, k=256, tiles=2, src=L["ckv"][:, 3:6, :], dst=(L["ckh"], L["ckl"]))
    L["meet"]()
    L["s_mla_project"]()
    if UPTO == 3:
        return fl("qm", 4096)
    if UPTO == 30:
        return fl("km", 4224)
    L["s_latent"]()
    if UPTO == 4:
        return fl("ymh", 4 * T, F32R)
    L["s_mix"]()
    mh_, ml_ = L["mixh"], L["mixl"]
    s_out("wout", (8,), lambda kt, i: (mh_[:, kt, :], ml_[:, kt, :]), T, 4, False)
    s_postnorm("p2", "mix_post", T, 1.0)
    if UPTO == 5:
        return fl("h", DT * TK)
    s_prenorm("n3", "ffn2_pre", T)
    s_gate_up("f2gu", "n3", T)
    s_out("f2dn", (6, 6, 5, 5), rhs_hid(T), T, 2, False)
    s_postnorm("p3", "ffn2_post", T, 0.5)
    if UPTO == 6:
        return fl("h", DT * TK)
    s_prenorm("n4", "norm_mix0", T)
    L["s_hyin"](L["s_hyif"]())
    L["s_rglru"]()
    L["s_mlstm"]()
    if UPTO == 7:
        return fl("yh", DT * T, F32R)
    yh_, yl_ = L["yh"], L["yl"]
    s_out("hyout", (8,), lambda kt, i: (yh_[:, kt, :], yl_[:, kt, :]), T, 4, True)
    if UPTO == 8:
        return fl("h", DT * TK)
    s_prenorm("n5", "norm_ffn0", T)
    L["s_conv_up"]("up0", "n5", 0)
    s_out("dn0", (8, 8, 8), rhs_hid(T), T, 4, True)
    L["s_ple_proj"](0, "ng0", "norm_ple0")
    L["s_ple_gate"](0, "ng0", False)
    if UPTO == 9:
        return fl("h", DT * TK)
    L["s_qkv"]()
    L["s_window"]()
    if UPTO == 10:
        return fl("ayh", DT * T, F32R)
    ayh_, ayl_ = L["ayh"], L["ayl"]
    s_out("atout", (8,), lambda kt, i: (ayh_[:, kt, :], ayl_[:, kt, :]), T, 4, True)
    if UPTO == 11:
        return fl("h", DT * TK)
    s_prenorm("n7", "norm_ffn1", T)
    L["s_conv_up"]("up1", "n7", 1)
    s_out("dn1", (8, 8, 8), rhs_hid(T), T, 4, True)
    L["s_ple_proj"](1, "ng1", "norm_ple1")
    L["s_ple_gate"](1, "ng1", True)


def by_tile(w, nt=P):
    k, n = w.shape
    a = w.reshape(k // P, P, n // nt, nt).transpose(2, 1, 0, 3)
    return a.reshape(n // nt, P, -1)


def gate_up_tiles(g, u):
    g, u = by_tile(g), by_tile(u)
    n, p, w = g.shape
    return np.stack([g.reshape(n // 2, 2, p, w), u.reshape(n // 2, 2, p, w)], 1).reshape(2 * n, p, w)


def columns(v, rows=P):
    return v.reshape(-1, P).T


def lay_out(a):
    w_in = a["w_in"][0]
    w = {}
    w["f1gu"] = gate_up_tiles(a["ffn1_w_gate"][0], a["ffn1_w_up"][0])
    w["f1dn"] = by_tile(a["ffn1_w_down"][0])
    w["win"] = np.concatenate([by_tile(w_in[:, 0:2176]), by_tile(w_in[:, 2176:2304]), by_tile(w_in[:, 2208:4256])])
    uq = a["w_uq"][0].reshape(3, P, 4, 2, 96).transpose(2, 1, 3, 0, 4)
    w["uq"] = uq.reshape(4, P, 576)
    ukv = a["w_ukv"][0].reshape(2, P, 2, 4, P).transpose(2, 1, 3, 0, 4)
    w["ukv"] = ukv.reshape(2, P, 1024)
    so = by_tile(a["w_sb_o"][0]).reshape(4, 2, P, 512).transpose(0, 2, 1, 3).reshape(4, P, 1024)
    mo = by_tile(a["w_mla_o"][0]).reshape(4, 2, P, 512).transpose(0, 2, 1, 3).reshape(4, P, 1024)
    w["wo"] = np.stack([so, mo], 1).reshape(8, P, 1024)
    w["wout"] = by_tile(a["w_out"][0])
    w["f2gu"] = gate_up_tiles(a["ffn2_w_gate"][0], a["ffn2_w_up"][0])
    w["f2dn"] = by_tile(a["ffn2_w_down"][0])
    hy = a["hy_w_in_2"][0]
    w["hyin"] = by_tile(hy[:, 0:3072])
    w["hyif"] = by_tile(hy[:, 3072:3080], 8)
    w["hyout"] = by_tile(a["hy_w_out_2"][0])
    for i in range(2):
        w[f"up{i}"] = gate_up_tiles(a["ff_w_up_2"][i][:, 0:FF2], a["ff_w_up_2"][i][:, FF2:])
        dn = by_tile(a["ff_w_down_2"][i]).reshape(DT, P, 3, SLOT).transpose(0, 2, 1, 3)
        w[f"dn{i}"] = dn.reshape(3 * DT, P, SLOT)
        w[f"pp{i}"] = by_tile(a["ple_w_proj_2"][i]).reshape(2, 4, P, 256).transpose(0, 2, 1, 3).reshape(2, P, SLOT)
        w[f"pg{i}"] = by_tile(a["ple_w_gate_2"][i])
    w["qkv"] = by_tile(a["at_w_qkv_2"][0])
    w["atout"] = by_tile(a["at_w_out_2"][0])
    out = {"w_" + k: np.ascontiguousarray(v) for k, v in w.items()}

    tokens = np.concatenate([a["x"][0], a["meta_tokens"]], 0)
    out["xT"] = np.ascontiguousarray(tokens.T.reshape(DT, P, TK))
    out["pT"] = np.ascontiguousarray(a["p_2"][:, 0].transpose(0, 2, 1).reshape(2, 2, P, T))
    out["pos"] = np.ascontiguousarray(a["positions_2"].astype(a["positions_2"].dtype))
    out["rw"] = np.ascontiguousarray(np.stack([a["rg_w_a_2"][0], a["rg_w_x_2"][0]]))

    vec = np.zeros((P, NVEC), np.float32)

    def put(name, cols):
        vec[0:cols.shape[0], VOFF[name]:VOFF[name] + cols.shape[1]] = cols

    for name, key, i in [("ffn1_pre", "ffn1_pre_g", 0), ("ffn1_post", "ffn1_post_g", 0), ("mix_pre", "mix_pre_g", 0),
                         ("b_gate", "b_gate", 0), ("q_norm", "q_norm_g", 0), ("kv_norm", "kv_norm_g", 0),
                         ("mix_post", "mix_post_g", 0), ("ffn2_pre", "ffn2_pre_g", 0),
                         ("ffn2_post", "ffn2_post_g", 0), ("norm_mix0", "norm_mix_2", 0), ("norm_mix1", "norm_mix_2", 1),
                         ("norm_ffn0", "norm_ffn_2", 0), ("norm_ffn1", "norm_ffn_2", 1),
                         ("norm_ple0", "norm_ple_2", 0), ("norm_ple1", "norm_ple_2", 1),
                         ("rg_cb", "rg_conv_b_2", 0), ("rg_ba", "rg_b_a_2", 0), ("rg_bx", "rg_b_x_2", 0),
                         ("rg_lam", "rg_lambda_2", 0), ("ml_cb", "ml_conv_b_2", 0), ("ml_norm", "ml_norm_2", 0),
                         ("ff_cb0", "ff_conv_b_2", 0), ("ff_cb1", "ff_conv_b_2", 1)]:
        put(name, columns(a[key][i]))
    hb = a["hy_b_in_2"][0]
    put("hy_b", columns(hb[0:3072]))
    put("b_i", hb[3072:3076][:, None])
    put("b_f", hb[3076:3080][:, None])
    put("rg_cw", np.concatenate([columns(a["rg_conv_w_2"][0][t]) for t in range(4)], 1))
    put("ml_cw", np.concatenate([columns(a["ml_conv_w_2"][0][t]) for t in range(4)], 1))
    for i in range(2):
        put(f"ff_cw{i}", np.concatenate([columns(a["ff_conv_w_2"][i][t]) for t in range(3)], 1))
    put("at_qn", np.tile(a["at_q_norm_2"][0], 2)[:, None])
    put("at_kn", np.tile(a["at_k_norm_2"][0], 2)[:, None])
    by_place = a["at_sinks_2"][0].reshape(4, 2, 2).transpose(0, 2, 1).reshape(16)
    put("sinks", np.broadcast_to(by_place[None, :], (P, 16)))
    out["vec"] = vec
    out.update(shape_constants())
    return out


def shape_constants():
    con = np.zeros((P, NCON), np.float32)

    def put(name, m):
        con[0:m.shape[0], COFF[name]:COFF[name] + m.shape[1]] = m
    i = np.arange(P)
    put("ident", np.eye(P))
    put("ones", np.ones((P, P)))
    put("tri", -(i[:, None] >= i[None, :]).astype(np.float32))
    put("negones", -np.ones((P, P)))
    m = np.zeros((P, P))
    for k in range(16):
        m[80 + k, 64 + k] = -1.0
        m[64 + k, 80 + k] = 1.0
    put("permm", m)
    m = np.zeros((P, P))
    for b in (0, 64):
        for k in range(32):
            m[b + 32 + k, b + k] = -1.0
            m[b + k, b + 32 + k] = 1.0
    put("permh", m)
    put("blk64", (i[:, None] // 64 == i[None, :] // 64).astype(np.float32))
    for b in (0, 1):
        put(f"dup{b}", (i[:, None] == 64 * b + i[None, :] % 64).astype(np.float32))
    m = np.zeros((4, 4, P))
    for k in range(4):
        m[k, k, :] = 1.0
    put("sel", m.reshape(4, 512))
    kj = np.arange(2 * P)
    put("band", np.where((kj[None, :] > i[:, None]) & (kj[None, :] <= i[:, None] + P), 0.0, NEG))
    inv = np.float32(10000.0) ** (-np.arange(32, dtype=np.float32) * np.float32(2.0 / 64))
    put("invf", np.tile(inv, 4)[:, None])
    out = {"con": con}
    pos = np.concatenate([np.arange(META, TK), np.arange(META)]).astype(np.float32)
    inv = np.float32(10000.0) ** (-np.arange(16, dtype=np.float32) / np.float32(16))
    ang = (pos[None, :] * inv[:, None]).astype(np.float32)
    out["rope"] = np.ascontiguousarray(np.stack([np.tile(np.cos(ang), (2, 1)), np.tile(np.sin(ang), (2, 1))]).astype(np.float32))
    return out


def kernel(**inputs):
    import concourse.bacc as _bacc
    from concourse.bass_utils import run_bass_kernel_spmd as _run

    arrays = lay_out({k: np.asarray(v) for k, v in inputs.items()})
    nc = _bacc.Bacc("TRN2", target_bir_lowering=False, num_devices=1, dynamic_dma_scratch_size=1024)
    d, maps = {}, {}
    for name, v in arrays.items():
        maps[name + "_dram"] = v
        d[name] = nc.dram_tensor(name + "_dram", v.shape, mybir.dt.from_np(v.dtype), kind="ExternalInput").ap()
    oshape = (DT, P, T) if UPTO == 99 else (P, 8448)
    out = nc.dram_tensor("out_dram", oshape, F32, kind="ExternalOutput").ap()
    program(nc, d, out)
    r = _run(nc, [maps], core_ids=[0])
    got = r.results[0]["out_dram"]
    return np.ascontiguousarray(got.reshape(D, T).T).reshape(1, T, D) if UPTO == 99 else got
```
